# Optimizing a Trainium2 kernel written in Bass

```python
import jax, jax.numpy as jnp
from jax import lax
import numpy as np
import math
import jax
import jax.numpy as jnp

D_MODEL = 1024
BATCH = 1
SEQ = 512
DEPTH = 1

GRID_W = 64
CTX_LEN = 256
D_MIX = D_MODEL
C_CONV = D_MIX // 2
CONV_K = 31
N_HEADS = 8
QK_NOPE = 64
QK_ROPE = 32
V_DIM = 64
Q_LORA = 384
KV_LORA = 256
D_FF = 2816
FFN_K = 3
Q_BLOCK = 128
ROPE_THETA = 10000.0
LN_EPS = 1e-5
ALPHA = (2 * DEPTH) ** 0.25
BETA = (8 * DEPTH) ** -0.25
D_IN = 2 * C_CONV + Q_LORA + KV_LORA + QK_ROPE
SOFTMAX_SCALE = (QK_NOPE + QK_ROPE) ** -0.5


def layer_norm(x, g=None, b=None):
    xf = x.astype(jnp.float32)
    mu = xf.mean(-1, keepdims=True)
    var = jnp.square(xf - mu).mean(-1, keepdims=True)
    y = (xf - mu) * lax.rsqrt(var + LN_EPS)
    if g is not None:
        y = y * g.astype(jnp.float32) + b.astype(jnp.float32)
    return y.astype(x.dtype)

def rms_norm(x, g):
    xf = x.astype(jnp.float32)
    y = xf * lax.rsqrt(jnp.square(xf).mean(-1, keepdims=True) + LN_EPS) * g.astype(jnp.float32)
    return y.astype(x.dtype)

def dwconv(x, w, b):
    k = w.shape[0]
    y = lax.conv_general_dilated(x, w[:, None, :], window_strides=(1,),
                                 padding=[(k // 2, k // 2)],
                                 dimension_numbers=('NWC', 'WIO', 'NWC'),
                                 feature_group_count=x.shape[-1])
    return y + b

def axial_rope_tables(n, dtype):
    rows = n // GRID_W
    row = jnp.repeat(jnp.arange(rows), GRID_W)
    col = jnp.tile(jnp.arange(GRID_W), rows)
    n_freq = QK_ROPE // 4
    inv = ROPE_THETA ** (-jnp.arange(n_freq, dtype=jnp.float32) / n_freq)
    ang = jnp.concatenate([row[:, None] * inv, col[:, None] * inv], axis=-1)
    return jnp.cos(ang).astype(dtype), jnp.sin(ang).astype(dtype)

def apply_rope(x, cos, sin):
    half = x.shape[-1] // 2
    x1, x2 = x[..., :half], x[..., half:]
    return jnp.concatenate([x1 * cos - x2 * sin, x2 * cos + x1 * sin], axis=-1)

def mixer_inputs(h, w_in):
    z = h @ w_in
    return jnp.split(z, [2 * C_CONV, 2 * C_CONV + Q_LORA, 2 * C_CONV + Q_LORA + KV_LORA], axis=-1)

def conformer_conv(u, dw_w, dw_b, ln_g, ln_b):
    a, gte = jnp.split(u, 2, axis=-1)
    v = a * jax.nn.sigmoid(gte)
    v = dwconv(v, dw_w, dw_b)
    return jax.nn.silu(layer_norm(v, ln_g, ln_b))

def mla_queries(cq, q_norm_g, w_uq, cos, sin):
    b, n = cq.shape[:2]
    q = (rms_norm(cq, q_norm_g) @ w_uq).reshape(b, n, N_HEADS, QK_NOPE + QK_ROPE)
    q_nope, q_rope = q[..., :QK_NOPE], q[..., QK_NOPE:]
    if cos is not None:
        q_rope = apply_rope(q_rope, cos[:, None, :], sin[:, None, :])
    return q_nope, q_rope

def mla_keys_values(ckv, kr, kv_norm_g, w_ukv, cos, sin):
    b, n = ckv.shape[:2]
    kv = (rms_norm(ckv, kv_norm_g) @ w_ukv).reshape(b, n, N_HEADS, QK_NOPE + V_DIM)
    k_nope, v = kv[..., :QK_NOPE], kv[..., QK_NOPE:]
    k_rope = kr if cos is None else apply_rope(kr, cos, sin)
    return k_nope, k_rope, v

def attend(q_nope, q_rope, k_nope, k_rope, v):
    s = (jnp.einsum('bqhd,bkhd->bhqk', q_nope, k_nope)
         + jnp.einsum('bqhr,bkr->bhqk', q_rope, k_rope)).astype(jnp.float32) * SOFTMAX_SCALE
    p = jax.nn.softmax(s, axis=-1).astype(v.dtype)
    return jnp.einsum('bhqk,bkhd->bqhd', p, v)

def attend_blocked(q_nope, q_rope, k_nope, k_rope, v):
    b, n = q_nope.shape[:2]
    nb = n // Q_BLOCK
    qn = q_nope.reshape(b, nb, Q_BLOCK, N_HEADS, QK_NOPE).transpose(1, 0, 2, 3, 4)
    qr = q_rope.reshape(b, nb, Q_BLOCK, N_HEADS, QK_ROPE).transpose(1, 0, 2, 3, 4)
    out = lax.map(lambda qs: attend(qs[0], qs[1], k_nope, k_rope, v), (qn, qr))
    return out.transpose(1, 0, 2, 3, 4).reshape(b, n, N_HEADS, V_DIM)

def merge_groups(conv_out, attn_out, w_o, b_o):
    b, n = conv_out.shape[:2]
    cat = jnp.concatenate([conv_out, attn_out.reshape(b, n, N_HEADS * V_DIM)], axis=-1)
    return cat @ w_o + b_o

def conv_ffn(h, w_up, dw_w, dw_b, w_down, b_down):
    u = dwconv(h @ w_up, dw_w, dw_b)
    g, val = jnp.split(u, 2, axis=-1)
    return (jax.nn.silu(g) * val) @ w_down + b_down

def first_inputs(seed: int = 0) -> dict:
    key = jax.random.key(seed)
    ks = jax.random.split(key, 32)
    L = DEPTH

    def nrm(k, shape, s):
        return s * jax.random.normal(k, shape, jnp.float32)

    return {
        'x': nrm(ks[0], (BATCH, SEQ, D_MODEL), 1.0),
        'c': nrm(ks[1], (BATCH, D_MODEL), 1.0),
        'ctx': nrm(ks[2], (BATCH, CTX_LEN, D_MODEL), 1.0),
        'c_ctx': nrm(ks[3], (D_MODEL,), 1.0),
        'w_ada': nrm(ks[4], (L, D_MODEL, 6 * D_MODEL), D_MODEL ** -0.5),
        'b_ada': nrm(ks[5], (L, 6 * D_MODEL), 0.02),
        'w_in': nrm(ks[6], (L, D_MODEL, D_IN), D_MODEL ** -0.5),
        'conv_dw_w': nrm(ks[7], (L, CONV_K, C_CONV), CONV_K ** -0.5),
        'conv_dw_b': nrm(ks[8], (L, C_CONV), 0.02),
        'conv_ln_g': 1.0 + nrm(ks[9], (L, C_CONV), 0.05),
        'conv_ln_b': nrm(ks[10], (L, C_CONV), 0.02),
        'q_norm_g': 1.0 + nrm(ks[11], (L, Q_LORA), 0.05),
        'w_uq': nrm(ks[12], (L, Q_LORA, N_HEADS * (QK_NOPE + QK_ROPE)), Q_LORA ** -0.5),
        'kv_norm_g': 1.0 + nrm(ks[13], (L, KV_LORA), 0.05),
        'w_ukv': nrm(ks[14], (L, KV_LORA, N_HEADS * (QK_NOPE + V_DIM)), KV_LORA ** -0.5),
        'w_o': nrm(ks[15], (L, D_MIX, D_MODEL), BETA * D_MIX ** -0.5),
        'b_o': nrm(ks[16], (L, D_MODEL), 0.02),
        'ln1_g': 1.0 + nrm(ks[17], (L, D_MODEL), 0.05),
        'ln1_b': nrm(ks[18], (L, D_MODEL), 0.02),
        'w_up': nrm(ks[19], (L, D_MODEL, 2 * D_FF), D_MODEL ** -0.5),
        'ffn_dw_w': nrm(ks[20], (L, FFN_K, 2 * D_FF), FFN_K ** -0.5),
        'ffn_dw_b': nrm(ks[21], (L, 2 * D_FF), 0.02),
        'w_down': nrm(ks[22], (L, D_FF, D_MODEL), BETA * D_FF ** -0.5),
        'b_down': nrm(ks[23], (L, D_MODEL), 0.02),
        'ln2_g': 1.0 + nrm(ks[24], (L, D_MODEL), 0.05),
        'ln2_b': nrm(ks[25], (L, D_MODEL), 0.02),
    }

def first_block(x, c, ctx, c_ctx, w_ada, b_ada, w_in, conv_dw_w, conv_dw_b, conv_ln_g, conv_ln_b,
              q_norm_g, w_uq, kv_norm_g, w_ukv, w_o, b_o, ln1_g, ln1_b,
              w_up, ffn_dw_w, ffn_dw_b, w_down, b_down, ln2_g, ln2_b):
    n = x.shape[1]
    cos, sin = axial_rope_tables(n, x.dtype)
    x = layer_norm(x)
    ctx = layer_norm(ctx)
    for i in range(DEPTH):
        last = i == DEPTH - 1
        mod = jax.nn.silu(c) @ w_ada[i] + b_ada[i]
        sh1, sc1, g1, sh2, sc2, g2 = jnp.split(mod[:, None, :], 6, axis=-1)
        modc = jax.nn.silu(c_ctx) @ w_ada[i] + b_ada[i]
        sh1c, sc1c, g1c, sh2c, sc2c, g2c = jnp.split(modc, 6)

        u_c, cq_c, ckv_c, kr_c = mixer_inputs(ctx * (1 + sc1c) + sh1c, w_in[i])
        k_nope_c, k_rope_c, v_c = mla_keys_values(ckv_c, kr_c, kv_norm_g[i], w_ukv[i], None, None)

        u_l, cq_l, ckv_l, kr_l = mixer_inputs(x * (1 + sc1) + sh1, w_in[i])
        k_nope_l, k_rope_l, v_l = mla_keys_values(ckv_l, kr_l, kv_norm_g[i], w_ukv[i], cos, sin)
        q_nope_l, q_rope_l = mla_queries(cq_l, q_norm_g[i], w_uq[i], cos, sin)
        attn_l = attend_blocked(q_nope_l, q_rope_l,
                                jnp.concatenate([k_nope_c, k_nope_l], axis=1),
                                jnp.concatenate([k_rope_c, k_rope_l], axis=1),
                                jnp.concatenate([v_c, v_l], axis=1))
        conv_l = conformer_conv(u_l, conv_dw_w[i], conv_dw_b[i], conv_ln_g[i], conv_ln_b[i])
        y_l = merge_groups(conv_l, attn_l, w_o[i], b_o[i])
        x_mid = layer_norm(ALPHA * x + g1 * y_l, ln1_g[i], ln1_b[i])

        if not last:
            q_nope_c, q_rope_c = mla_queries(cq_c, q_norm_g[i], w_uq[i], None, None)
            attn_c = attend(q_nope_c, q_rope_c, k_nope_c, k_rope_c, v_c)
            conv_c = conformer_conv(u_c, conv_dw_w[i], conv_dw_b[i], conv_ln_g[i], conv_ln_b[i])
            y_c = merge_groups(conv_c, attn_c, w_o[i], b_o[i])
            ctx = layer_norm(ALPHA * ctx + g1c * y_c, ln1_g[i], ln1_b[i])
            f_c = conv_ffn(ctx * (1 + sc2c) + sh2c, w_up[i], ffn_dw_w[i], ffn_dw_b[i], w_down[i], b_down[i])
            ctx = layer_norm(ALPHA * ctx + g2c * f_c, ln2_g[i], ln2_b[i])

        f_l = conv_ffn(x_mid * (1 + sc2) + sh2, w_up[i], ffn_dw_w[i], ffn_dw_b[i], w_down[i], b_down[i])
        x = layer_norm(ALPHA * x_mid + g2 * f_l, ln2_g[i], ln2_b[i])
    return x


F32 = jnp.float32
RMS_EPS = 1e-6
N_ATTN_HEADS = 8
ATTN_HEAD_DIM = 64
ATTN_W = N_ATTN_HEADS * ATTN_HEAD_DIM
IDX_HEADS = 16
IDX_DIM = 32
IDX_Q = IDX_HEADS * IDX_DIM
TOPK_MAX = 256
Q_BLOCK_2 = 64
N_BUCKETS = 32
MAX_DISTANCE = 128
RWKV_HEADS = 8
RWKV_HEAD = 64
RWKV_W = RWKV_HEADS * RWKV_HEAD
DECAY_LORA = 64
ICLR_LORA = 64
GATE_LORA = 128
RWKV_IN = 3 * RWKV_W + DECAY_LORA + ICLR_LORA + GATE_LORA
GN_EPS = 64e-5
RWKV_START = 3 * ATTN_W + IDX_Q + IDX_DIM + IDX_HEADS
N_IN = RWKV_START + RWKV_IN + 2 * D_MODEL
IN_SPLITS = (ATTN_W, 2 * ATTN_W, 3 * ATTN_W, 3 * ATTN_W + IDX_Q,
             3 * ATTN_W + IDX_Q + IDX_DIM, RWKV_START,
             RWKV_START + RWKV_IN, RWKV_START + RWKV_IN + D_MODEL)
RWKV_SPLITS = (RWKV_W, 2 * RWKV_W, 3 * RWKV_W, 3 * RWKV_W + DECAY_LORA,
               3 * RWKV_W + DECAY_LORA + ICLR_LORA)
N_EXPERTS = 64
N_GROUPS = 8
TOPK_GROUPS = 4
MOE_TOPK = 8
EXPERT_FF = 256
ROUTED_SCALE = 2.5
EXPERT_BLOCK = 128


def rms_norm_2(x, g):
    xf = x.astype(F32)
    y = xf * lax.rsqrt(jnp.mean(xf * xf, axis=-1, keepdims=True) + RMS_EPS)
    return (y * g.astype(F32)).astype(x.dtype)

def t5_bucket(rel):
    n = jnp.maximum(rel, 0)
    max_exact = N_BUCKETS // 2
    nf = jnp.maximum(n, 1).astype(F32)
    large = max_exact + (jnp.log(nf / max_exact) / math.log(MAX_DISTANCE / max_exact)
                         * (N_BUCKETS - max_exact)).astype(jnp.int32)
    large = jnp.minimum(large, N_BUCKETS - 1)
    return jnp.where(n < max_exact, n, large)

def dsa_sparse_attention(q, k, v, q_idx, k_idx, w_idx, rel_bias):
    B, S = q.shape[0], q.shape[1]
    top_k = min(TOPK_MAX, S // 4)
    nb = S // Q_BLOCK_2
    k_flat = k.reshape(B, S, ATTN_W)
    v_flat = v.reshape(B, S, ATTN_W)
    key_pos = jnp.arange(S, dtype=jnp.int32)
    idx_scale = (IDX_HEADS ** -0.5) * (IDX_DIM ** -0.5)

    def to_blocks(t):
        return jnp.moveaxis(t.reshape((B, nb, Q_BLOCK_2) + t.shape[2:]), 1, 0)

    def block(args):
        qb, qib, wib, start = args
        q_pos = start + jnp.arange(Q_BLOCK_2, dtype=jnp.int32)
        dots = jnp.einsum('bqhd,bsd->bqhs', qib, k_idx, preferred_element_type=F32)
        idx_score = jnp.einsum('bqhs,bqh->bqs', jax.nn.relu(dots), wib.astype(F32)) * idx_scale
        causal = key_pos[None, :] <= q_pos[:, None]
        idx_score = jnp.where(causal[None], idx_score, -jnp.inf)
        _, sel = lax.top_k(idx_score, top_k)
        kg = jax.vmap(lambda kf, i: kf[i])(k_flat, sel).reshape(B, Q_BLOCK_2, top_k, N_ATTN_HEADS, ATTN_HEAD_DIM)
        vg = jax.vmap(lambda vf, i: vf[i])(v_flat, sel).reshape(B, Q_BLOCK_2, top_k, N_ATTN_HEADS, ATTN_HEAD_DIM)
        logits = jnp.einsum('bqhd,bqkhd->bqhk', qb, kg, preferred_element_type=F32) * (ATTN_HEAD_DIM ** -0.5)
        rel = q_pos[None, :, None] - sel
        bias = rel_bias[t5_bucket(rel)].astype(F32)
        logits = logits + jnp.moveaxis(bias, -1, 2)
        valid = sel <= q_pos[None, :, None]
        logits = jnp.where(valid[:, :, None, :], logits, -jnp.inf)
        p = jax.nn.softmax(logits, axis=-1).astype(vg.dtype)
        return jnp.einsum('bqhk,bqkhd->bqhd', p, vg)

    starts = jnp.arange(nb, dtype=jnp.int32) * Q_BLOCK_2
    out = lax.map(block, (to_blocks(q), to_blocks(q_idx), to_blocks(w_idx), starts))
    return jnp.moveaxis(out, 0, 1).reshape(B, S, ATTN_W)

def wkv7_scan(r, decay, k, v, a, b):
    B, S, H, N = r.shape

    def step(state, inp):
        r_t, w_t, k_t, v_t, a_t, b_t = inp
        sa = jnp.einsum('bhij,bhj->bhi', state, a_t)
        state = state * w_t[:, :, None, :] + sa[..., None] * b_t[:, :, None, :] + v_t[..., None] * k_t[:, :, None, :]
        y = jnp.einsum('bhij,bhj->bhi', state, r_t)
        return state, y

    xs = tuple(jnp.moveaxis(t, 1, 0) for t in (r, decay, k, v, a, b))
    _, ys = lax.scan(step, jnp.zeros((B, H, N, N), F32), xs)
    return jnp.moveaxis(ys, 0, 1)

def rwkv7_branch(z, tshift_mu, decay_w0, decay_up, iclr_a0, iclr_up, gate_up, k_k, k_a, r_k, lnx_g, lnx_b):
    B, S = z.shape[0], z.shape[1]
    z_prev = jnp.pad(z[:, :-1], ((0, 0), (1, 0), (0, 0)))
    z = (z + tshift_mu * (z_prev - z)).astype(F32)
    r, k, v, wd, ad, gd = jnp.split(z, RWKV_SPLITS, axis=-1)
    w_log = -jax.nn.softplus(-(decay_w0.astype(F32) + jnp.tanh(wd) @ decay_up.astype(F32))) - 0.5
    decay = jnp.exp(-jnp.exp(w_log))
    a = jax.nn.sigmoid(iclr_a0.astype(F32) + ad @ iclr_up.astype(F32))
    g = jax.nn.sigmoid(gd) @ gate_up.astype(F32)
    heads = lambda t: t.reshape(B, S, RWKV_HEADS, RWKV_HEAD)
    kk = heads(k * k_k.astype(F32))
    kk = kk / jnp.maximum(jnp.sqrt(jnp.sum(kk * kk, axis=-1, keepdims=True)), 1e-12)
    k = k * (1.0 + (a - 1.0) * k_a.astype(F32))
    r, k, v, decay, a = heads(r), heads(k), heads(v), heads(decay), heads(a)
    y = wkv7_scan(r, decay, k, v, -kk, kk * a)
    mu = jnp.mean(y, axis=-1, keepdims=True)
    var = jnp.mean(jnp.square(y - mu), axis=-1, keepdims=True)
    yn = ((y - mu) * lax.rsqrt(var + GN_EPS)).reshape(B, S, RWKV_W)
    yn = yn * lnx_g.astype(F32) + lnx_b.astype(F32)
    bonus = (jnp.sum(r * k * r_k.astype(F32), axis=-1, keepdims=True) * v).reshape(B, S, RWKV_W)
    return (yn + bonus) * g

def swiglu(h, wg, wu, wd):
    return (jax.nn.silu(h @ wg) * (h @ wu)) @ wd

def moe_ffn(h, router_w, router_bias, exp_gate, exp_up, exp_down, sh_gate, sh_up, sh_down):
    B, S, D = h.shape
    T = B * S
    hf = h.reshape(T, D)
    scores = jax.nn.sigmoid(jnp.einsum('td,de->te', hf, router_w, preferred_element_type=F32))
    choice = scores + router_bias.astype(F32)
    grp_score = lax.top_k(choice.reshape(T, N_GROUPS, N_EXPERTS // N_GROUPS), 2)[0].sum(-1)
    _, top_g = lax.top_k(grp_score, TOPK_GROUPS)
    gmask = jnp.any(top_g[:, :, None] == jnp.arange(N_GROUPS)[None, None, :], axis=1)
    emask = jnp.repeat(gmask, N_EXPERTS // N_GROUPS, axis=1)
    _, top_e = lax.top_k(jnp.where(emask, choice, -jnp.inf), MOE_TOPK)
    gw = jnp.take_along_axis(scores, top_e, axis=1)
    gw = gw / jnp.sum(gw, axis=-1, keepdims=True) * ROUTED_SCALE
    A = T * MOE_TOPK
    flat_e = top_e.reshape(A)
    order = jnp.argsort(flat_e)
    se = flat_e[order]
    counts = jnp.bincount(flat_e, length=N_EXPERTS)
    padded = (counts + EXPERT_BLOCK - 1) // EXPERT_BLOCK * EXPERT_BLOCK
    start = jnp.cumsum(counts) - counts
    pend = jnp.cumsum(padded)
    pstart = pend - padded
    dest = pstart[se] + jnp.arange(A, dtype=jnp.int32) - start[se]
    n_blocks = -(-A // EXPERT_BLOCK) + N_EXPERTS
    P = n_blocks * EXPERT_BLOCK
    slot_tok = jnp.zeros((P,), jnp.int32).at[dest].set((order // MOE_TOPK).astype(jnp.int32))
    slot_w = jnp.zeros((P,), F32).at[dest].set(gw.reshape(A)[order])
    block_start = jnp.arange(n_blocks, dtype=jnp.int32) * EXPERT_BLOCK
    block_e = jnp.minimum(jnp.sum(pend[None, :] <= block_start[:, None], axis=1), N_EXPERTS - 1)

    def step(y, blk):
        tok, wt, e = blk
        out = swiglu(hf[tok], exp_gate[e], exp_up[e], exp_down[e])
        return y.at[tok].add(out.astype(F32) * wt[:, None]), None

    y, _ = lax.scan(step, jnp.zeros((T, D), F32),
                    (slot_tok.reshape(n_blocks, EXPERT_BLOCK), slot_w.reshape(n_blocks, EXPERT_BLOCK), block_e))
    shared = swiglu(hf, sh_gate, sh_up, sh_down)
    return (y.astype(h.dtype) + shared).reshape(B, S, D)

def hybrid_layer(x, c, ada_w, ada_b, norm1_g, w_in, rel_bias, tshift_mu, decay_w0, decay_up,
                 iclr_a0, iclr_up, gate_up, k_k, k_a, r_k, lnx_g, lnx_b, w_attn_br, w_rwkv_br,
                 w_out, norm2_g, router_w, router_bias, exp_gate, exp_up, exp_down,
                 sh_gate, sh_up, sh_down):
    B, S, D = x.shape
    mod = (jax.nn.silu(c.astype(F32)) @ ada_w.astype(F32) + ada_b.astype(F32)).astype(x.dtype)
    sh1, sc1, g1, sh2, sc2, g2 = [m[:, None, :] for m in jnp.split(mod, 6, axis=-1)]
    h = rms_norm_2(x, norm1_g) * (1 + sc1) + sh1
    z = h @ w_in
    q, k, v, iq, ik, iw, zr, ga, gr = jnp.split(z, IN_SPLITS, axis=-1)
    hs = lambda t: t.reshape(B, S, N_ATTN_HEADS, ATTN_HEAD_DIM)
    attn = dsa_sparse_attention(hs(q), hs(k), hs(v), iq.reshape(B, S, IDX_HEADS, IDX_DIM), ik, iw, rel_bias)
    rw = rwkv7_branch(zr, tshift_mu, decay_w0, decay_up, iclr_a0, iclr_up, gate_up,
                      k_k, k_a, r_k, lnx_g, lnx_b).astype(x.dtype)
    mixed = jax.nn.sigmoid(ga) * (attn @ w_attn_br) + jax.nn.sigmoid(gr) * (rw @ w_rwkv_br)
    x = x + g1 * (mixed @ w_out)
    h2 = rms_norm_2(x, norm2_g) * (1 + sc2) + sh2
    x = x + g2 * moe_ffn(h2, router_w, router_bias, exp_gate, exp_up, exp_down, sh_gate, sh_up, sh_down)
    return x

def second_inputs(seed: int = 0) -> dict:
    key = jax.random.key(seed)
    ks = iter(jax.random.split(key, 40))
    L, D = DEPTH, D_MODEL

    def nrm(shape, scale):
        return jax.random.normal(next(ks), shape, F32) * scale

    def uni(shape, lo, hi):
        return jax.random.uniform(next(ks), shape, F32, lo, hi)

    return {
        'x': nrm((BATCH, SEQ, D), 1.0),
        'c': nrm((BATCH, D), 1.0),
        'ada_w': nrm((L, D, 6 * D), 0.5 * D ** -0.5),
        'ada_b': nrm((L, 6 * D), 0.02),
        'norm1_g': 1.0 + nrm((L, D), 0.02),
        'w_in': nrm((L, D, N_IN), D ** -0.5),
        'rel_bias': nrm((N_BUCKETS, N_ATTN_HEADS), 0.5),
        'tshift_mu': uni((L, RWKV_IN), 0.0, 1.0),
        'decay_w0': uni((L, RWKV_W), -3.0, 1.0),
        'decay_up': nrm((L, DECAY_LORA, RWKV_W), 0.1),
        'iclr_a0': nrm((L, RWKV_W), 0.5),
        'iclr_up': nrm((L, ICLR_LORA, RWKV_W), ICLR_LORA ** -0.5),
        'gate_up': nrm((L, GATE_LORA, RWKV_W), GATE_LORA ** -0.5),
        'k_k': 0.85 + nrm((L, RWKV_W), 0.02),
        'k_a': 1.0 + nrm((L, RWKV_W), 0.02),
        'r_k': nrm((L, RWKV_HEADS, RWKV_HEAD), 0.1),
        'lnx_g': 1.0 + nrm((L, RWKV_W), 0.02),
        'lnx_b': nrm((L, RWKV_W), 0.02),
        'w_attn_br': nrm((L, ATTN_W, D), ATTN_W ** -0.5),
        'w_rwkv_br': nrm((L, RWKV_W, D), RWKV_W ** -0.5),
        'w_out': nrm((L, D, D), D ** -0.5),
        'norm2_g': 1.0 + nrm((L, D), 0.02),
        'router_w': nrm((L, D, N_EXPERTS), D ** -0.5),
        'router_bias': nrm((L, N_EXPERTS), 0.01),
        'exp_gate': nrm((L, N_EXPERTS, D, EXPERT_FF), D ** -0.5),
        'exp_up': nrm((L, N_EXPERTS, D, EXPERT_FF), D ** -0.5),
        'exp_down': nrm((L, N_EXPERTS, EXPERT_FF, D), EXPERT_FF ** -0.5),
        'sh_gate': nrm((L, D, EXPERT_FF), D ** -0.5),
        'sh_up': nrm((L, D, EXPERT_FF), D ** -0.5),
        'sh_down': nrm((L, EXPERT_FF, D), EXPERT_FF ** -0.5),
        'final_g': 1.0 + nrm((D,), 0.02),
    }

def second_block(x, c, ada_w, ada_b, norm1_g, w_in, rel_bias, tshift_mu, decay_w0, decay_up,
              iclr_a0, iclr_up, gate_up, k_k, k_a, r_k, lnx_g, lnx_b, w_attn_br, w_rwkv_br,
              w_out, norm2_g, router_w, router_bias, exp_gate, exp_up, exp_down,
              sh_gate, sh_up, sh_down, final_g):
    for l in range(DEPTH):
        x = hybrid_layer(x, c, ada_w[l], ada_b[l], norm1_g[l], w_in[l], rel_bias, tshift_mu[l],
                         decay_w0[l], decay_up[l], iclr_a0[l], iclr_up[l], gate_up[l], k_k[l],
                         k_a[l], r_k[l], lnx_g[l], lnx_b[l], w_attn_br[l], w_rwkv_br[l], w_out[l],
                         norm2_g[l], router_w[l], router_bias[l], exp_gate[l], exp_up[l],
                         exp_down[l], sh_gate[l], sh_up[l], sh_down[l])
    return rms_norm_2(x, final_g)


def setup_inputs(seed=0):
    out = dict(first_inputs(seed))
    for name, value in second_inputs(seed + 1).items():
        if name != "x":
            out[name + "_2"] = value
    return out


def reference(
    x, c, ctx, c_ctx, w_ada, b_ada, w_in, conv_dw_w, conv_dw_b, conv_ln_g, conv_ln_b, q_norm_g,
    w_uq, kv_norm_g, w_ukv, w_o, b_o, ln1_g, ln1_b, w_up, ffn_dw_w, ffn_dw_b, w_down, b_down,
    ln2_g, ln2_b, c_2, ada_w_2, ada_b_2, norm1_g_2, w_in_2, rel_bias_2, tshift_mu_2, decay_w0_2,
    decay_up_2, iclr_a0_2, iclr_up_2, gate_up_2, k_k_2, k_a_2, r_k_2, lnx_g_2, lnx_b_2,
    w_attn_br_2, w_rwkv_br_2, w_out_2, norm2_g_2, router_w_2, router_bias_2, exp_gate_2,
    exp_up_2, exp_down_2, sh_gate_2, sh_up_2, sh_down_2, final_g_2,
):
    x = first_block(
        x, c, ctx, c_ctx, w_ada, b_ada, w_in, conv_dw_w, conv_dw_b, conv_ln_g, conv_ln_b,
        q_norm_g, w_uq, kv_norm_g, w_ukv, w_o, b_o, ln1_g, ln1_b, w_up, ffn_dw_w, ffn_dw_b,
        w_down, b_down, ln2_g, ln2_b,
    )
    return second_block(
        x, c_2, ada_w_2, ada_b_2, norm1_g_2, w_in_2, rel_bias_2, tshift_mu_2, decay_w0_2,
        decay_up_2, iclr_a0_2, iclr_up_2, gate_up_2, k_k_2, k_a_2, r_k_2, lnx_g_2, lnx_b_2,
        w_attn_br_2, w_rwkv_br_2, w_out_2, norm2_g_2, router_w_2, router_bias_2, exp_gate_2,
        exp_up_2, exp_down_2, sh_gate_2, sh_up_2, sh_down_2, final_g_2,
    )


_drawn_inputs = setup_inputs


def setup_inputs(seed=0):
    import zlib

    import numpy as np

    out = dict(_drawn_inputs(seed))
    spreads = {}
    factors = {'conv_dw_b': 3.715,
     'conv_ln_b': 4.115,
     'q_norm_g': 5.28,
     'kv_norm_g': 3.186,
     'norm1_g_2': 3.768,
     'k_k_2': 64.0,
     'k_a_2': 5.123,
     'lnx_g_2': 36.528,
     'lnx_b_2': 44.16,
     'final_g_2': 7.494,
     'conv_ln_g': 2.814,
     'rel_bias_2': 5.876,
     'decay_up_2': 4.434,
     'norm2_g_2': 8.0,
     'router_bias_2': 7.524}
    for name, (base, spread) in spreads.items():
        noise = np.random.default_rng([zlib.crc32(name.encode()), seed]).standard_normal(out[name].shape)
        drawn = base * np.exp(spread * noise) if base else spread * noise
        out[name] = jnp.asarray(drawn.astype(out[name].dtype))
    for name, factor in factors.items():
        out[name] = (out[name] * factor).astype(out[name].dtype)
    return out
```

```python
from contextlib import ExitStack

import numpy as np
import concourse.bass as bass
from concourse import mybir

F32 = mybir.dt.float32
I32 = mybir.dt.int32
U32 = mybir.dt.uint32
ALU = mybir.AluOpType
ACT = mybir.ActivationFunctionType
AX = mybir.AxisListType

P = 128
D = 1024
KD = D // P
T = 512
NT = T // P
CTX = 256
NCT = CTX // P
KEYS = CTX + T
NKT = KEYS // P
C_CONV, CONV_K = 512, 31
PAD = CONV_K // 2
HEADS, QK_NOPE, QK_ROPE, V_DIM = 8, 64, 32, 64
Q_LORA, KV_LORA = 384, 256
KQ, KKV = Q_LORA // P, KV_LORA // P
D_FF = 2816
NF = D_FF // P
LN_EPS, RMS_EPS, GN_EPS = 1e-5, 1e-6, 64e-5
ALPHA = 2.0 ** 0.25
MLA_SCALE = (QK_NOPE + QK_ROPE) ** -0.5
WS_COLS = 4096
ARENA = 52800
MOD = 6 * KD
SH1, SC1, G1, SH2, SC2, G2 = (KD * i for i in range(6))

COLS = {}


def _lay(names):
    at = 0
    for name, n in names:
        COLS[name] = at
        at += n
    return at


NCOLS = _lay([
    ("c", KD), ("c_ctx", KD), ("c_2", KD), ("b_ada", MOD),
    ("conv_dw_w", 4 * CONV_K), ("conv_dw_b", 4), ("conv_ln_g", 4), ("conv_ln_b", 4),
    ("q_norm_g", KQ), ("kv_norm_g", KKV), ("ln1_g", KD), ("ln1_b", KD),
    ("norm1_g_2", KD), ("tshift_mu_2", 14), ("decay_w0_2", 4), ("iclr_a0_2", 4),
    ("k_k_2", 4), ("k_a_2", 4), ("r_k_2", 4), ("lnx_g_2", 4), ("lnx_b_2", 4),
])
ROWS = ["b_o", "ln1_g", "ln1_b", "b_down", "ln2_g", "ln2_b", "final_g_2"]


class Signal:

    def __init__(self, nc, ctx, name):
        self.sem, self.n = ctx.enter_context(nc.semaphore(name)), 0

    def by(self, instruction, step=1):
        instruction.then_inc(self.sem, step)
        self.n += step
        return self.n


def link(engine, instruction, signal):
    engine.wait_ge(signal.sem, signal.by(instruction))


class Program:
    pass


class Memory:

    def __init__(self, tensor, size):
        self.tensor, self.free, self.place = tensor, [(0, size)], {}

    def buffer(self, name, shape):
        n = -(-int(np.prod(shape[1:])) // 8) * 8
        for i, (at, size) in enumerate(self.free):
            if size >= n:
                self.free[i] = (at + n, size - n)
                break
        else:
            raise MemoryError(f"no room for {name}: {n} of {self.free}")
        self.place[name] = (at, n, shape)
        ap = self.tensor[0:shape[0], at:at + int(np.prod(shape[1:]))]
        if len(shape) == 3:
            ap = ap.rearrange("p (a b) -> p a b", b=shape[2])
        if len(shape) == 4:
            ap = ap.rearrange("p (a b c) -> p a b c", b=shape[2], c=shape[3])
        return ap

    def release(self, *names):
        for name in names:
            at, n, _ = self.place[name]
            self.free.append((at, n))
        merged = []
        for at, n in sorted(x for x in self.free if x[1]):
            if merged and merged[-1][0] + merged[-1][1] == at:
                merged[-1] = (merged[-1][0], merged[-1][1] + n)
            else:
                merged.append((at, n))
        self.free = merged


def setup(nc, ctx, dram):
    K = Program()
    K.dram = dram

    arena = ctx.enter_context(nc.sbuf_tensor("arena", [P, ARENA], F32))
    K.memory = Memory(arena, ARENA)
    K.dma_signal = lambda name: Signal(nc, ctx, name)
    sb = K.buffer = K.memory.buffer

    K.flag = lambda name: Signal(nc, ctx, name)
    K.ident = sb("ident", [P, P])
    K.ones = sb("ones", [P, P])
    K.cols = sb("cols", [P, NCOLS])
    K.ws = sb("ws", [P, 2, WS_COLS])
    K.mod = sb("mod", [P, MOD, 2])
    K.fold = sb("fold", [P, 8, KD])
    K.res = sb("res", [P, NT, D])
    K.row = sb("row", [P, 4, D])
    K.stats = sb("stats", [P, 6, 2, 6])
    K.mv = sb("mv", [P, 6, 2])
    K.rstd = sb("rstd", [P, 6])
    K.psum = ctx.enter_context(nc.psum_tensor("psum", [P, 8 * 512], F32))
    K.bank = [K.psum[:, 512 * i:512 * i + 512] for i in range(8)]
    K.ws_landed = [K.flag(f"ws_landed{i}") for i in range(2)]
    K.ws_issued = 0
    K.ws_freed = []
    K.ws_taken = 0
    K.act_step = K.flag("act_step")
    K.dve_step = K.flag("dve_step")
    K.pool_step = K.flag("pool_step")
    K.rows_landed = K.flag("rows_landed")
    return K


def new_signals(nc, K, owner, ctx):
    sems = K.own
    if sems:
        with nc.Block() as block:
            @block.gpsimd
            def _(pool):
                nums = sorted(x.sem.num for x in sems)
                first = nums[0]
                for a, b in zip(nums, nums[1:] + [None]):
                    if b != a + 1:
                        pool.sem_clear(range(first, a + 1))
                        first = b
        owner.close()
    K.own = []
    K.ws_freed = [None] * len(K.ws_freed)

    def signal(name):
        K.own.append(Signal(nc, owner, name))
        return K.own[-1]
    K.flag = signal


def col(K, name, i=0, n=1):
    return K.cols[:, COLS[name] + i:COLS[name] + i + n]


def stream(K, sp, src):
    n = K.ws_issued
    if n >= 2 and K.ws_freed[n - 2]:
        sp.wait_ge(*K.ws_freed[n - 2])
    K.ws_landed[n % 2].by(sp.dma_start(K.ws[:, n % 2, 0:src.shape[1]], src), 16)
    K.ws_issued += 1


def stream_loop(K, sp, tiles, count, used):
    base = K.ws_issued
    stream(K, sp, tiles[0])
    stream(K, sp, tiles[1])
    with sp.Fori(1, count // 2) as i:
        for s in range(2):
            sp.wait_ge(used, i * 2 + (s - 1))
            src = tiles[bass.ds(i * 2 + s, 1)].rearrange("a p n -> (a p) n")
            sp.dma_start(K.ws[:, (base + s) % 2, 0:src.shape[1]], src).then_inc(K.ws_landed[(base + s) % 2].sem, 16)
    for s in range(2):
        K.ws_landed[(base + s) % 2].n += 16 * (count // 2 - 1)
    K.ws_issued += count - 2


def take(K, pe):
    n = K.ws_taken
    pe.wait_ge(K.ws_landed[n % 2].sem, 16 * (n // 2 + 1))
    K.ws_taken += 1
    return K.ws[:, n % 2, :]


def take_in_loop(K, pe, i, s):
    n = K.ws_taken + s
    pe.wait_ge(K.ws_landed[n % 2].sem, i * 16 + 16 * (n // 2 + 1))
    return K.ws[:, n % 2, :]


def free(K, signal, value=None):
    K.ws_freed.append((signal.sem, signal.n if value is None else value))


def spread(K, queue, slot, row):
    K.rows_landed.by(queue.dma_start(K.row[:, slot, :], row.partition_broadcast(P)), 16)


def norm_stats(K, dve, src, j, step):
    for half in range(2):
        link(dve, dve.bn_stats(K.stats[:, j, half, :], src[:, 512 * half:512 * half + 512]), step)
    link(dve, dve.bn_aggr(K.mv[:, j, :], K.stats[:, j, :, :].rearrange("p a b -> p (a b)")), step)


def phase_modulate(nc, K, ctx):
    d, sb = K.dram, K.buffer
    K.h1 = K.buffer("h1", [P, KD, KEYS])
    stage = sb("ada_w_stage", [P, 4, WS_COLS])
    cx = sb("cx", [P, NCT, D])
    silu_c = K.silu_c = sb("silu_c", [P, KD, 3])
    small, xin = K.flag("small_landed"), K.flag("x_landed")
    landed = [K.flag(f"ada_landed{i}") for i in range(4)]
    used = K.flag("ada_used")
    silu = K.flag("silu_c_done")
    summed = K.flag("ada_summed")
    ready = K.flag("mod_ready")
    var, root = K.flag("var_ready"), K.flag("root_ready")
    normed = K.flag("x_normed")
    turned = K.flag("x_turned")
    moved = K.flag("h1_written")
    gates, gates_sb = K.flag("gates_turned"), K.flag("gates_copied")
    gates_out = K.gates_out = K.flag("gates_in_dram")
    gt = sb("gt", [2 * KD, P])
    sum_bank = K.bank[0][:, 0:2 * MOD].rearrange("p (m v) -> p m v", v=2)

    with nc.Block() as block:
        @block.tensor
        def _(pe):
            pe.wait_ge(silu.sem, 1)
            with pe.Fori(0, 3) as i:
                for s in range(4):
                    pe.wait_ge(landed[s].sem, i * 16 + 16)
                    w = stage[:, s, :].rearrange("p (k m) -> p k m", k=KD)
                    for b in range(4):
                        for k in range(KD):
                            last = pe.matmul(K.bank[0][:, bass.ds(i * 32 + (8 * s + 2 * b), 2)], w[:, k, P * b:P * b + P],
                                             silu_c[:, k, 0:2], start=(k == 0), stop=(k == KD - 1))
                    last.then_inc(used.sem, 1)
            used.n += 12
            pe.wait_ge(normed.sem, 6)
            for n in range(2 * KD):
                k, part = n // 2, n % 2
                bank = K.bank[2 + n % 4]
                if n >= 4:
                    pe.wait_ge(moved.sem, n - 3)
                src, tiles = ((cx, NCT), (K.res, NT))[part]
                for t in range(tiles):
                    last = pe.transpose(bank[:, P * t:P * t + P], src[:, t, P * k:P * k + P], K.ident[:, :])
                turned.by(last)
            pe.wait_ge(ready.sem, 1)
            gates.by(pe.transpose(K.bank[6][0:2 * KD, 0:P], K.fold[:, 6:8, :].rearrange("p a k -> p (a k)"), K.ident[:, :]))

        @block.sync
        def _(sp):
            small.by(sp.dma_start(K.cols[:, :], d["cols"]), 16)
            small.by(sp.dma_start(K.ident[:, :], d["ident"]), 16)
            for s in range(4):
                landed[s].by(sp.dma_start(stage[:, s, :], d["w_ada"][s]), 16)
            xin.by(sp.dma_start(K.res[:, :, :], d["x"].rearrange("(t p) n -> p t n", p=P)), 16)
            xin.by(sp.dma_start(cx[:, :, :], d["ctx"].rearrange("(t p) n -> p t n", p=P)), 16)
            with sp.Fori(1, 3) as i:
                for s in range(4):
                    sp.wait_ge(used.sem, i * 4 + (s - 3))
                    src = d["w_ada"][bass.ds(i * 4 + s, 1)].rearrange("a p n -> (a p) n")
                    sp.dma_start(stage[:, s, :], src).then_inc(landed[s].sem, 16)
            stream(K, sp, d["w_in"][0])
            stream(K, sp, d["w_in"][1])
            sp.wait_ge(gates_sb.sem, 1)
            gates_out.by(sp.dma_start(d["gate_rows"][0], gt[:, :]), 16)

        @block.scalar
        def _(act):
            act.wait_ge(small.sem, 32)
            for v, name in enumerate(("c", "c_ctx", "c_2")):
                last = act.activation(silu_c[:, :, v], col(K, name, 0, KD), ACT.Silu)
            silu.by(last)
            act.wait_ge(var.sem, 1)
            root.by(act.activation(K.rstd[:, :], K.rstd[:, :], ACT.Sqrt))
            act.wait_ge(ready.sem, 1)
            for n in range(2 * KD):
                k, part = n // 2, n % 2
                act.wait_ge(turned.sem, n + 1)
                lo, size = ((0, CTX), (CTX, T))[part]
                moved.by(act.activation(K.h1[:, k, lo:lo + size], K.bank[2 + n % 4][:, 0:size], ACT.Identity,
                                        bias=K.mod[:, SH1 + k, 1 - part:2 - part], scale=K.mod[:, SC1 + k, 1 - part:2 - part]))
            act.wait_ge(gates.sem, 1)
            gates_sb.by(act.activation(gt[:, :], K.bank[6][0:2 * KD, 0:P], ACT.Copy))

        @block.gpsimd
        def _(pool):
            pool.memset(K.ones[:, :], 1.0)

        @block.vector
        def _(dve):
            dve.wait_ge(xin.sem, 32)
            tiles = [K.res[:, t, :] for t in range(NT)] + [cx[:, t, :] for t in range(NCT)]
            for j, x in enumerate(tiles):
                norm_stats(K, dve, x, j, K.dve_step)
            link(dve, dve.tensor_scalar(K.rstd[:, :], K.mv[:, :, 1], LN_EPS, None, ALU.add), var)
            dve.wait_ge(root.sem, 1)
            link(dve, dve.reciprocal(K.rstd[:, :], K.rstd[:, :]), K.dve_step)
            for j, x in enumerate(tiles):
                normed.by(dve.tensor_scalar(x, x, K.mv[:, j, 0:1], K.rstd[:, j:j + 1], ALU.subtract, ALU.mult))
            dve.wait_ge(used.sem, 12)
            for v in range(2):
                link(dve, dve.tensor_tensor(K.mod[:, :, v], sum_bank[:, :, v], col(K, "b_ada", 0, MOD), ALU.add), K.dve_step)
            link(dve, dve.tensor_scalar(K.mod[:, SC1:SC1 + KD, :], K.mod[:, SC1:SC1 + KD, :], 1.0, None, ALU.add), K.dve_step)
            link(dve, dve.tensor_scalar(K.fold[:, 0, :], K.mod[:, SC2:SC2 + KD, 0], 1.0, None, ALU.add), K.dve_step)
            link(dve, dve.tensor_tensor(K.fold[:, 1, :], K.fold[:, 0, :], col(K, "ln1_b", 0, KD), ALU.mult), K.dve_step)
            link(dve, dve.tensor_tensor(K.fold[:, 1, :], K.fold[:, 1, :], K.mod[:, SH2:SH2 + KD, 0], ALU.add), K.dve_step)
            link(dve, dve.tensor_tensor(K.fold[:, 0, :], K.fold[:, 0, :], col(K, "ln1_g", 0, KD), ALU.mult), K.dve_step)
            link(dve, dve.tensor_copy(K.fold[:, 6, :], K.mod[:, G1:G1 + KD, 0]), K.dve_step)
            link(dve, dve.tensor_copy(K.fold[:, 7, :], K.mod[:, G2:G2 + KD, 0]), ready)
    K.memory.release("ada_w_stage", "cx", "gt")


def phase_project(nc, K, ctx):
    d = K.dram
    sb = K.buffer
    K.vpad = sb("vpad", [P, 4, T + 2 * PAD])
    K.cq = sb("cq", [P, KQ, T])
    K.ckv = sb("ckv", [P, KKV, KEYS])
    K.kr = sb("kr", [P, KEYS])
    K.rope = sb("rope", [P, 2, T])
    sg, krs = sb("sg", [P, 4, T]), sb("krs", [P, T])
    rope_in = K.flag("rope_landed")
    aw, part = sb("ada2_stage", [P, 2, WS_COLS]), sb("ada2_part", [P, 12, 512])
    K.arow = sb("arow", [P, 4, D])
    a2in = [K.dma_signal("ada2_landed0"), K.dma_signal("ada2_landed1")]
    a2set, a2add, a2mm, a2row = (K.flag(n) for n in ("ada2_zeroed", "ada2_added", "ada2_summed", "ada2_rows"))
    a2bias = K.dma_signal("ada2_bias")
    sh_sc = aw[:, 0, 0:4 * 512].rearrange("p (a n) -> p a n", a=4)
    a2turn, n2in = K.flag("ada2_turned"), K.dma_signal("norm2_g_landed")
    gate_mm, a_mm = K.flag("glu_gate_summed"), K.flag("glu_a_summed")
    gate_sb, a_sb = K.flag("glu_gate_out"), K.flag("glu_a_out")
    rest_mm, rest_sb = K.flag("latents_summed"), K.flag("latents_out")

    latents = [(2, P * k, CTX, T, K.cq[:, k, :]) for k in range(KQ)]
    for k in range(KKV):
        latents += [(3, P * k, 0, CTX, K.ckv[:, k, 0:CTX]), (3, P * k, CTX, T, K.ckv[:, k, CTX:KEYS])]
    latents += [(3, 2 * P, 0, CTX, K.kr[:, 0:CTX]), (3, 2 * P, CTX, T, K.kr[:, CTX:KEYS]), (3, 3 * P, CTX, T, krs[:, :])]

    with nc.Block() as block:
        @block.tensor
        def _(pe):
            for half in range(2):
                w = take(K, pe).rearrange("p (k m) -> p k m", k=KD)
                for b in range(4):
                    if half:
                        pe.wait_ge(gate_sb.sem, b + 1)
                    for k in range(KD):
                        last = pe.matmul(K.bank[b][:, :], w[:, k, P * b:P * b + P], K.h1[:, k, CTX:KEYS], start=(k == 0), stop=(k == KD - 1))
                    (a_mm if half else gate_mm).by(last)
                free(K, a_mm if half else gate_mm)
            now = None
            for n, (tile, c, lo, size, _) in enumerate(latents):
                if tile != now:
                    w, now = take(K, pe), tile
                    cols_ = Q_LORA if tile == 2 else 4 * P
                    w = w[:, 0:KD * cols_].rearrange("p (k m) -> p k m", k=KD)
                if n >= 4:
                    pe.wait_ge(rest_sb.sem, n - 3)
                for k in range(KD):
                    last = pe.matmul(K.bank[4 + n % 4][:, 0:size], w[:, k, c:c + P], K.h1[:, k, lo:lo + size], start=(k == 0), stop=(k == KD - 1))
                rest_mm.by(last)
                if n + 1 == len(latents) or latents[n + 1][0] != tile:
                    free(K, rest_mm)
            pe.wait_ge(a2add.sem, 16 + 12 * KD)
            for n in range(12):
                if n < 4:
                    pe.wait_ge(a_sb.sem, n + 1)
                else:
                    pe.wait_ge(a2row.sem, n - 3)
                a2mm.by(pe.matmul(K.bank[n % 4], K.ones[:, :], part[:, n, :], start=True, stop=True))
            pe.wait_ge(a2row.sem, 12)
            for n in range(2 * KD):
                last = pe.transpose(K.bank[n // 4][:, P * (n % 4):P * (n % 4) + P], sh_sc[:, n // 4, P * (n % 4):P * (n % 4) + P], K.ident[:, :])
            a2turn.by(last)

        @block.sync
        def _(sp):
            rope_in.by(sp.dma_start(K.rope[:, :, :], d["rope"]), 16)
            for tile in (d["w_in"][2][:, 0:KD * Q_LORA], d["w_in"][3], d["w_uq"], d["w_ukv"]):
                stream(K, sp, tile)

        @block.scalar
        def _(act):
            for b in range(4):
                act.wait_ge(gate_mm.sem, b + 1)
                gate_sb.by(act.activation(sg[:, b, :], K.bank[b][:, :], ACT.Sigmoid))
            for n, (_, _, _, size, out) in enumerate(latents):
                act.wait_ge(rest_mm.sem, n + 1)
                rest_sb.by(act.activation(out, K.bank[4 + n % 4][:, 0:size], ACT.Copy))
            for n in range(12):
                act.wait_ge(a2mm.sem, n + 1)
                dst = sh_sc[:, n, :] if n < 4 else K.arow[:, n // 2 - 2, 512 * (n % 2):512 * (n % 2) + 512]
                a2row.by(act.activation(dst, K.bank[n % 4], ACT.Copy))

        @block.gpsimd
        def _(pool):
            pool.wait_ge(K.gates_out.sem, 16)
            link(pool, pool.memset(part[:, :, :], 0.0), a2set)
            a2bias.by(pool.dma_start(part[0:1, :, :], d["ada_b_2"]), 16)
            with pool.Fori(0, 6) as i:
                for s in range(2):
                    pool.wait_ge(a2add.sem, i * 16 + (8 * s + 8))
                    src = d["ada_w_2"][bass.ds(i * 2 + s, 1)].rearrange("a p n -> (a p) n")
                    pool.dma_start(aw[:, s, :], src).then_inc(a2in[s].sem, 16)
            n2in.by(pool.dma_start(K.row[:, 0, :], d["norm2_g"].partition_broadcast(P)), 16)
            pool.memset(K.vpad[:, :, 0:PAD], 0.0)
            pool.memset(K.vpad[:, :, PAD + T:], 0.0)

        @block.vector
        def _(dve):
            dve.sem_inc(a2add.sem, 16)
            dve.wait_ge(a2bias.sem, 16)
            with dve.Fori(0, 6) as i:
                for s in range(2):
                    dve.wait_ge(a2in[s].sem, i * 16 + 16)
                    to = part[:, bass.ds(i * 2 + s, 1), :].rearrange("p a n -> p (a n)")
                    for k in range(KD):
                        dve.scalar_tensor_tensor(out=to, in0=aw[:, s, 512 * k:512 * k + 512], scalar=K.silu_c[:, k, 2:3], in1=to,
                                                 op0=ALU.mult, op1=ALU.add).then_inc(a2add.sem, 1)
                        dve.wait_ge(a2add.sem, i * 16 + (8 * s + k + 17))
            for b in range(4):
                dve.wait_ge(gate_sb.sem, b + 1)
                dve.wait_ge(a_mm.sem, b + 1)
                a_sb.by(dve.tensor_tensor(K.vpad[:, b, PAD:PAD + T], K.bank[b][:, :], sg[:, b, :], ALU.mult))
            dve.wait_ge(rope_in.sem, 16)
            dve.wait_ge(rest_sb.sem, len(latents))
            link(dve, dve.tensor_tensor(krs[:, :], krs[:, :], K.rope[:, 1, :], ALU.mult), K.dve_step)
            link(dve, dve.tensor_tensor(K.kr[:, CTX:KEYS], K.kr[:, CTX:KEYS], K.rope[:, 0, :], ALU.mult), K.dve_step)
            link(dve, dve.tensor_tensor(K.kr[:, CTX:KEYS], K.kr[:, CTX:KEYS], krs[:, :], ALU.add), K.dve_step)
            dve.wait_ge(a2row.sem, 12)
            dve.wait_ge(n2in.sem, 16)
            link(dve, dve.tensor_scalar(K.arow[:, 2, :], K.arow[:, 2, :], 1.0, None, ALU.add), K.dve_step)
            link(dve, dve.tensor_tensor(K.arow[:, 2, :], K.arow[:, 2, :], K.row[:, 0, :], ALU.mult), K.dve_step)
            dve.wait_ge(a2turn.sem, 1)
            turned = K.psum[:, 0:2 * D].rearrange("p (v k c) -> p v k c", v=2, k=KD)
            link(dve, dve.tensor_copy(K.fold[:, 3, :], turned[:, 0, :, 0]), K.dve_step)
            link(dve, dve.tensor_scalar(K.fold[:, 2, :], turned[:, 1, :, 0], 1.0, None, ALU.add), K.dve_step)
            link(dve, dve.tensor_tensor(K.fold[:, 2, :], K.fold[:, 2, :], col(K, "norm1_g_2", 0, KD), ALU.mult), K.dve_step)
    K.memory.release("h1", "sg", "krs", "ada2_stage", "ada2_part", "silu_c")


def phase_mix(nc, K, ctx):
    d = K.dram
    sb = K.buffer
    K.cat = sb("cat", [P, KD, T])
    sq = sb("sq", [P, 4, T])
    rs = sb("rs", [P, KEYS])
    qn, qr, qs = sb("qn", [P, 4, T]), sb("qr", [P, 2, T]), sb("qs", [P, 2, T])
    kn, v = sb("kn", [P, 4, KEYS]), sb("v", [P, NKT, 512])
    prob, probT = sb("prob", [P, 2, KEYS]), sb("probT", [P, 2, NKT, P])
    nmax, rsum, att = sb("nmax", [P, 32]), sb("rsum", [P, 32]), sb("att", [P, NT, 512])
    qz = [x.rearrange("p (part h t) -> p part h t", part=2, h=HEADS) for x in
          (K.row[:, 2:4, :].rearrange("p a n -> p (a n)"), sq[:, :, :].rearrange("p a t -> p (a t)"))]
    conv = K.cat[:, 0:4, :]
    sig = K.flag
    qz_zero, qz_in = sig("q_padded_zeroed"), sig("q_padded")
    sq_q, sq_kv, ss = sig("cq_squared"), sig("ckv_squared"), sig("squares_summed")
    ms, root = sig("mean_square"), sig("root_latent")
    latent = sig("latents_normed")
    mm, out = sig("qkv_summed"), sig("qkv_out")
    roped = sig("q_roped")
    s_mm, mx, ex = sig("scores"), sig("row_max"), sig("probs")
    t_pe, t_sb, pv, o_sb = sig("probs_turned"), sig("probsT_out"), sig("pv_summed"), sig("att_out")
    a_pe, a_sb = sig("att_turned"), sig("att_in_cat")
    tap = sig("conv_tap")
    mean_mm, cent, sq_c, var_mm, var, root_c, nrm = (sig(n) for n in (
        "conv_mean", "conv_centred", "conv_squared", "conv_var_summed", "conv_var", "conv_root", "conv_normed"))

    jobs = []
    wq = K.ws[:, K.ws_taken % 2, 0:KQ * 1024].rearrange("p (k m) -> p k m", k=KQ)
    wkv = K.ws[:, (K.ws_taken + 1) % 2, 0:KKV * 1024].rearrange("p (k m) -> p k m", k=KKV)
    for b in range(8):
        dst = qn[:, b, :] if b < 4 else qr[:, b - 4, :] if b < 6 else qs[:, b - 6, :]
        jobs.append((KQ, lambda k, b=b: (wq[:, k, P * b:P * b + P], K.cq[:, k, :]), T, dst, MLA_SCALE))
    for b in range(4):
        for lo, size in ((0, CTX), (CTX, T)):
            jobs.append((KKV, lambda k, b=b, lo=lo, size=size: (wkv[:, k, P * b:P * b + P], K.ckv[:, k, lo:lo + size]),
                         size, kn[:, b, lo:lo + size], 1.0))
    for t in range(NKT):
        jobs.append((KKV, lambda k, t=t: (K.ckv[:, k, P * t:P * t + P], wkv[:, k, 512:1024]), 512, v[:, t, :], 1.0))
    sum_banks = [(0, 0, T), (1, 0, CTX), (2, CTX, T)]
    UNITS = NT * HEADS
    S = [K.psum[:, 1024 * i:1024 * i + KEYS] for i in range(2)]
    PT = K.psum[:, 2048:2048 + KEYS]

    with nc.Block() as block:
        @block.tensor
        def _(pe):
            pe.wait_ge(sq_q.sem, 1)
            for k in range(KQ):
                last = pe.matmul(K.bank[0][:, :], K.ones[:, :], sq[:, k, :], start=(k == 0), stop=(k == KQ - 1))
            ss.by(last)
            for i, (bank, lo, size) in enumerate(((1, 0, CTX), (2, CTX, T))):
                pe.wait_ge(sq_kv.sem, i + 1)
                for k in range(KKV):
                    last = pe.matmul(K.bank[bank][:, 0:size], K.ones[:, :],
                                     (sq[:, 3, 0:512].rearrange("p (k n) -> p k n", k=2)[:, k, :] if i == 0 else sq[:, k, :]),
                                     start=(k == 0), stop=(k == KKV - 1))
                ss.by(last)
            take(K, pe)
            for n, (inner, operands, size, _, _) in enumerate(jobs):
                if n == 0:
                    pe.wait_ge(latent.sem, 1)
                if n == 8:
                    free(K, mm)
                    take(K, pe)
                    pe.wait_ge(latent.sem, 3)
                if n >= 5:
                    pe.wait_ge(out.sem, n - 4)
                for k in range(inner):
                    w, x = operands(k)
                    last = pe.matmul(K.bank[3 + n % 5][:, 0:size], w, x, start=(k == 0), stop=(k == inner - 1))
                mm.by(last)
            free(K, mm)
            pe.wait_ge(out.sem, len(jobs))
            pe.wait_ge(roped.sem, 2)

            def scores(n):
                qt, h = divmod(n, HEADS)
                if n >= 2:
                    pe.wait_ge(ex.sem, n - 1)
                if h == 0:
                    pe.wait_ge(qz_in.sem, 2 * HEADS * (qt + 1))
                for lo, size in ((0, 512), (512, KEYS - 512)):
                    pe.matmul(S[n % 2][:, lo:lo + size], qz[qt % 2][:, 0, h, :], kn[:, h // 2, lo:lo + size], start=True, stop=False)
                    last = pe.matmul(S[n % 2][:, lo:lo + size], qz[qt % 2][:, 1, h, :], K.kr[:, lo:lo + size], start=False, stop=True)
                s_mm.by(last)

            def turn(n):
                pe.wait_ge(ex.sem, n + 1)
                if n:
                    pe.wait_ge(t_sb.sem, n)
                for k in range(NKT):
                    last = pe.transpose(PT[:, P * k:P * k + P], prob[:, n % 2, P * k:P * k + P], K.ident[:, :])
                t_pe.by(last)

            def weigh(n):
                qt, h = divmod(n, HEADS)
                pe.wait_ge(t_sb.sem, n + 1)
                if h == 0 and qt:
                    pe.wait_ge(o_sb.sem, qt)
                for k in range(NKT):
                    last = pe.matmul(K.bank[6][:, 64 * h:64 * h + 64], probT[:, n % 2, k, :], v[:, k, 64 * h:64 * h + 64],
                                     start=(k == 0), stop=(k == NKT - 1))
                pv.by(last)

            for n in range(UNITS + 2):
                if n < UNITS:
                    scores(n)
                if 1 <= n <= UNITS:
                    turn(n - 1)
                if n >= 2:
                    weigh(n - 2)
            pe.wait_ge(tap.sem, 4 * CONV_K)
            for k in range(4):
                last = pe.matmul(K.bank[7][:, :], K.ones[:, :], conv[:, k, :], start=(k == 0), stop=(k == 3))
            mean_mm.by(last)
            pe.wait_ge(o_sb.sem, NT)
            for c in range(4):
                for t in range(NT):
                    last = pe.transpose(K.bank[c][:, P * t:P * t + P], att[:, t, P * c:P * c + P], K.ident[:, :])
                a_pe.by(last)
            pe.wait_ge(sq_c.sem, 4)
            for k in range(4):
                last = pe.matmul(K.bank[6][:, :], K.ones[:, :], sq[:, k, :], start=(k == 0), stop=(k == 3))
            var_mm.by(last)

        @block.sync
        def _(sp):
            stream(K, sp, d["w_o"][0])
            stream(K, sp, d["w_o"][1])

        @block.scalar
        def _(act):
            sq_q.by(act.activation(sq[:, 0:KQ, :], K.cq[:, :, :], ACT.Square))
            sq_kv.by(act.activation(sq[:, 3, 0:512].rearrange("p (k n) -> p k n", k=2), K.ckv[:, :, 0:CTX], ACT.Square))
            act.wait_ge(ss.sem, 1)
            sq_kv.by(act.activation(sq[:, 0:KKV, :], K.ckv[:, :, CTX:KEYS], ACT.Square))
            for i, (_, lo, size) in enumerate(sum_banks):
                act.wait_ge(ms.sem, i + 1)
                buf = sq[:, 2, :] if i == 0 else rs[:, lo:lo + size]
                root.by(act.activation(buf, buf, ACT.Sqrt))
            for n, (_, _, size, dst, scale) in enumerate(jobs):
                act.wait_ge(mm.sem, n + 1)
                out.by(act.activation(dst, K.bank[3 + n % 5][:, 0:size], ACT.Copy, scale=scale))

            def exps(n):
                act.wait_ge(mx.sem, n + 1)
                if n >= 2:
                    act.wait_ge(t_pe.sem, n - 1)
                ex.by(act.activation(prob[:, n % 2, :], S[n % 2], ACT.Exp, bias=nmax[:, n:n + 1], accum_out=rsum[:, n:n + 1]))

            def turned(n):
                act.wait_ge(t_pe.sem, n + 1)
                if n >= 2:
                    act.wait_ge(pv.sem, n - 1)
                t_sb.by(act.activation(probT[:, n % 2, :, :].rearrange("p k q -> p (k q)"), PT, ACT.Copy))

            for n in range(UNITS + 1):
                if n < UNITS:
                    exps(n)
                if n:
                    turned(n - 1)
            for k in range(4):
                act.wait_ge(cent.sem, k + 1)
                sq_c.by(act.activation(sq[:, k, :], conv[:, k, :], ACT.Square))
            for c in range(4):
                act.wait_ge(a_pe.sem, c + 1)
                a_sb.by(act.activation(K.cat[:, 4 + c, :], K.bank[c][:, :], ACT.Copy))
            act.wait_ge(var.sem, 1)
            root_c.by(act.activation(rs[:, 0:T], rs[:, 0:T], ACT.Sqrt))
            for k in range(4):
                act.wait_ge(nrm.sem, k + 1)
                act.activation(K.cat[:, k, :], conv[:, k, :], ACT.Silu, bias=col(K, "conv_ln_b", k), scale=col(K, "conv_ln_g", k))

        @block.gpsimd
        def _(pool):
            def pad(qt):
                if qt >= 2:
                    pool.wait_ge(s_mm.sem, HEADS * (qt - 1))
                for h in range(HEADS):
                    a, b = P // 2 * (h % 2), 32 * (h % 4)
                    link(pool, pool.tensor_copy(qz[qt % 2][a:a + 64, 0, h, :], qn[a:a + 64, h // 2, P * qt:P * qt + P]), qz_in)
                    link(pool, pool.tensor_copy(qz[qt % 2][b:b + 32, 1, h, :], qr[b:b + 32, h // 4, P * qt:P * qt + P]), qz_in)

            link(pool, pool.memset(qz[0], 0.0), qz_zero)
            pool.wait_ge(latent.sem, 3)
            link(pool, pool.memset(qz[1], 0.0), qz_zero)
            pool.wait_ge(out.sem, len(jobs))
            pool.wait_ge(roped.sem, 2)
            for qt in range(NT):
                pad(qt)
            pool.wait_ge(K.gates_out.sem, 16)
            spread(K, pool, 0, d["gate_rows"][0, 0:KD, :].rearrange("k p -> (k p)"))
            spread(K, pool, 1, d["rows"][ROWS.index("b_o")])
            pool.wait_ge(K.rows_landed.sem, K.rows_landed.n)
            link(pool, pool.tensor_tensor(K.row[:, 1, :], K.row[:, 0, :], K.row[:, 1, :], ALU.mult), K.pool_step)
            for t in range(NT):
                link(pool, pool.tensor_scalar(K.res[:, t, :], K.res[:, t, :], ALPHA, 0.0, ALU.mult, ALU.add), K.pool_step)
                link(pool, pool.tensor_tensor(K.res[:, t, :], K.res[:, t, :], K.row[:, 1, :], ALU.add), K.pool_step)

        @block.vector
        def _(dve):
            for i, (bank, lo, size) in enumerate(sum_banks):
                dve.wait_ge(ss.sem, i + 1)
                buf = sq[:, 2, :] if i == 0 else rs[:, lo:lo + size]
                width = Q_LORA if i == 0 else KV_LORA
                ms.by(dve.tensor_scalar(buf, K.bank[bank][:, 0:size], 1.0 / width, LN_EPS, ALU.mult, ALU.add))
            for i, (bank, lo, size) in enumerate(sum_banks):
                dve.wait_ge(root.sem, i + 1)
                buf = sq[:, 2, :] if i == 0 else rs[:, lo:lo + size]
                link(dve, dve.reciprocal(buf, buf), K.dve_step)
                for k in range(KKV if i else KQ):
                    x = K.ckv[:, k, lo:lo + size] if i else K.cq[:, k, :]
                    g = col(K, "kv_norm_g" if i else "q_norm_g", k)
                    link(dve, dve.scalar_tensor_tensor(out=x, in0=x, scalar=g, in1=buf, op0=ALU.mult, op1=ALU.mult),
                         latent if k == (KKV if i else KQ) - 1 else K.dve_step)
            dve.wait_ge(out.sem, 8)
            for t in range(2):
                link(dve, dve.tensor_tensor(qs[:, t, :], qs[:, t, :], K.rope[:, 1, :], ALU.mult), K.dve_step)
                link(dve, dve.tensor_tensor(qr[:, t, :], qr[:, t, :], K.rope[:, 0, :], ALU.mult), K.dve_step)
                link(dve, dve.tensor_tensor(qr[:, t, :], qr[:, t, :], qs[:, t, :], ALU.add), roped)

            def taps(n):
                for k in range(4):
                    x, w = K.vpad[:, k, n:n + T], col(K, "conv_dw_w", CONV_K * k + n)
                    if n == 0:
                        tap.by(dve.tensor_scalar(conv[:, k, :], x, w, col(K, "conv_dw_b", k), ALU.mult, ALU.add))
                    else:
                        dve.wait_ge(tap.sem, 4 * (n - 1) + k + 1)
                        tap.by(dve.scalar_tensor_tensor(out=conv[:, k, :], in0=x, scalar=w, in1=conv[:, k, :], op0=ALU.mult, op1=ALU.add))

            def row_max(n):
                dve.wait_ge(s_mm.sem, n + 1)
                mx.by(dve.tensor_reduce(nmax[:, n:n + 1], S[n % 2], AX.X, ALU.max, negate=True))

            def output(qt):
                dve.wait_ge(pv.sem, HEADS * (qt + 1))
                u = slice(HEADS * qt, HEADS * qt + HEADS)
                link(dve, dve.reciprocal(rsum[:, u], rsum[:, u]), K.dve_step)
                link(dve, dve.tensor_tensor(att[:, qt, :].rearrange("p (h v) -> p h v", h=HEADS),
                                            K.bank[6][:, :].rearrange("p (h v) -> p h v", h=HEADS),
                                            rsum[:, u].unsqueeze(2).to_broadcast([P, HEADS, 64]), ALU.mult), o_sb)

            for n in range(UNITS + 2):
                if n < UNITS:
                    row_max(n)
                if n < CONV_K:
                    taps(n)
                if n >= HEADS + 2 and (n - 2) % HEADS == 0:
                    output((n - 2) // HEADS - 1)
            output(NT - 1)
            dve.wait_ge(mean_mm.sem, 1)
            link(dve, dve.tensor_scalar(rs[:, 0:T], K.bank[7][:, :], 1.0 / C_CONV, None, ALU.mult), K.dve_step)
            for k in range(4):
                cent.by(dve.tensor_tensor(conv[:, k, :], conv[:, k, :], rs[:, 0:T], ALU.subtract))
            dve.wait_ge(cent.sem, 4)
            dve.wait_ge(var_mm.sem, 1)
            link(dve, dve.tensor_scalar(rs[:, 0:T], K.bank[6][:, :], 1.0 / C_CONV, LN_EPS, ALU.mult, ALU.add), var)
            dve.wait_ge(root_c.sem, 1)
            link(dve, dve.reciprocal(rs[:, 0:T], rs[:, 0:T]), K.dve_step)
            for k in range(4):
                nrm.by(dve.tensor_tensor(conv[:, k, :], conv[:, k, :], rs[:, 0:T], ALU.mult))
    K.memory.release("sq", "rs", "qn", "qr", "qs", "kn", "v", "prob", "probT", "nmax", "rsum", "att", "vpad", "cq", "ckv", "kr", "rope")


def project_tokens(K, pe, lhs, tiles, per, mm, before=None):
    slots = [take(K, pe).rearrange("p (k n) -> p k n", k=per) for _ in range(tiles)]
    for t in range(NT):
        for half in range(2):
            for k in range(per * tiles):
                last = pe.matmul(K.bank[2 * t + half], lhs[:, k, P * t:P * t + P], slots[k // per][:, k % per, 512 * half:512 * half + 512],
                                 start=(k == 0), stop=(k == per * tiles - 1))
        mm.by(last)
    for _ in range(tiles):
        free(K, mm)


def turn_channels(K, pe, src, wait, turned, moved):
    pe.wait_ge(*wait)
    for k in range(KD):
        if k >= 4:
            pe.wait_ge(moved.sem, moved.n + k - 3)
        for t in range(NT):
            last = pe.transpose(K.bank[k % 4][:, P * t:P * t + P], src[:, t, P * k:P * k + P], K.ident[:, :])
        turned.by(last)


def phase_output(nc, K, ctx):
    d, sb, sig = K.dram, K.buffer, K.flag
    K.h = sb("h", [P, KD, T])
    gated = sb("gated", [P, D])
    mm, var, root, normed = sig("w_o_summed"), sig("var_1"), sig("root_1"), sig("normed_1")
    turned, moved = sig("turned_1"), sig("h_written_1")

    with nc.Block() as block:
        @block.tensor
        def _(pe):
            project_tokens(K, pe, K.cat, 2, 4, mm)
            turn_channels(K, pe, K.res, (normed.sem, NT), turned, moved)

        @block.sync
        def _(sp):
            stream(K, sp, d["w_up"][0])
            stream(K, sp, d["w_up"][1])

        @block.vector
        def _(dve):
            for t in range(NT):
                dve.wait_ge(mm.sem, t + 1)
                link(dve, dve.tensor_tensor(gated[:, :], K.psum[:, D * t:D * t + D], K.row[:, 0, :], ALU.mult), K.dve_step)
                link(dve, dve.tensor_tensor(K.res[:, t, :], K.res[:, t, :], gated[:, :], ALU.add), K.dve_step)
                norm_stats(K, dve, K.res[:, t, :], t, K.dve_step)
                link(dve, dve.tensor_scalar(K.rstd[:, t:t + 1], K.mv[:, t, 1:2], LN_EPS, None, ALU.add), var)
                dve.wait_ge(root.sem, t + 1)
                link(dve, dve.reciprocal(K.rstd[:, t:t + 1], K.rstd[:, t:t + 1]), K.dve_step)
                normed.by(dve.tensor_scalar(K.res[:, t, :], K.res[:, t, :], K.mv[:, t, 0:1], K.rstd[:, t:t + 1], ALU.subtract, ALU.mult))

        @block.scalar
        def _(act):
            for t in range(NT):
                act.wait_ge(var.sem, t + 1)
                root.by(act.activation(K.rstd[:, t:t + 1], K.rstd[:, t:t + 1], ACT.Sqrt))
            for k in range(KD):
                act.wait_ge(turned.sem, k + 1)
                moved.by(act.activation(K.h[:, k, :], K.bank[k % 4], ACT.Identity, bias=K.fold[:, 1, k:k + 1], scale=K.fold[:, 0, k:k + 1]))
    K.memory.release("gated", "cat")


def phase_ffn_up(nc, K, ctx):
    d, sb, sig = K.dram, K.buffer, K.flag
    K.hmid = sb("hmid", [P, NF, T])
    taps = sb("ffn_taps", [P, 2, 8])
    conv = sb("ffn_conv", [P, 2, 2, T])
    par, summed, seed, conved, gated, done = (sig(n) for n in (
        "taps_landed", "up_summed", "centre_tap", "ffn_conved", "ffn_silu", "hmid_written"))
    par = [par, sig("taps_landed1")]

    with nc.Block() as block:
        @block.tensor
        def _(pe):
            with pe.Fori(0, NF // 2) as i:
                for s in range(2):
                    w = take_in_loop(K, pe, i, s)[:, 0:KD * 2 * P].rearrange("p (k m) -> p k m", k=KD)
                    pe.wait_ge(done.sem, i * 2 + (s + 1))
                    for half in range(2):
                        for k in range(KD):
                            last = pe.matmul(K.bank[2 * s + half], w[:, k, P * half:P * half + P], K.h[:, k, :], start=(k == 0), stop=(k == KD - 1))
                        last.then_inc(summed.sem, 1)
            K.ws_taken += NF
            for n in range(NF):
                K.ws_freed.append((summed.sem, 2 * n + 2))

        @block.sync
        def _(sp):
            base = K.ws_issued
            with sp.Fori(0, NF // 2 - 1) as i:
                for s in range(2):
                    sp.wait_ge(summed.sem, i * 4 + (2 * s + 2))
                    src = d["w_up"][bass.ds(i * 2 + (2 + s), 1)].rearrange("a p n -> (a p) n")
                    sp.dma_start(K.ws[:, (base + s) % 2, 0:src.shape[1]], src).then_inc(K.ws_landed[(base + s) % 2].sem, 16)
            for s in range(2):
                K.ws_landed[(base + s) % 2].n += 16 * (NF // 2 - 1)
            K.ws_issued += NF - 2
            stream(K, sp, d["w_down"][0])
            stream(K, sp, d["w_down"][1])

        @block.scalar
        def _(act):
            with act.Fori(0, NF // 2) as i:
                for s in range(2):
                    act.wait_ge(done.sem, i * 2 + (s + 1))
                    act.dma_start(taps[:, s, :], d["ffn_taps"][bass.ds(i * 2 + s, 1)].rearrange("a p n -> (a p) n")).then_inc(par[s].sem, 16)
                for s in range(2):
                    act.wait_ge(par[s].sem, i * 16 + 16)
                    for half in range(2):
                        act.wait_ge(summed.sem, i * 4 + (2 * s + half + 1))
                        act.activation(conv[:, s, half, :], K.bank[2 * s + half], ACT.Identity, bias=taps[:, s, 4 * half + 3:4 * half + 4],
                                       scale=taps[:, s, 4 * half + 1:4 * half + 2]).then_inc(seed.sem, 1)
                for s in range(2):
                    act.wait_ge(conved.sem, i * 8 + (4 * s + 2))
                    act.activation(conv[:, s, 0, :], conv[:, s, 0, :], ACT.Silu).then_inc(gated.sem, 1)

        @block.vector
        def _(dve):
            dve.sem_inc(done.sem, 2)
            with dve.Fori(0, NF // 2) as i:
                for s in range(2):
                    for half in range(2):
                        dve.wait_ge(seed.sem, i * 4 + (2 * s + half + 1))
                        c, u = conv[:, s, half, :], K.bank[2 * s + half]
                        for n, (to, fr, tap) in enumerate(((slice(1, T), slice(0, T - 1), 0), (slice(0, T - 1), slice(1, T), 2))):
                            dve.scalar_tensor_tensor(out=c[:, to], in0=u[:, fr], scalar=taps[:, s, 4 * half + tap:4 * half + tap + 1], in1=c[:, to],
                                                     op0=ALU.mult, op1=ALU.add).then_inc(conved.sem, 1)
                            dve.wait_ge(conved.sem, i * 8 + (4 * s + 2 * half + n + 1))
                for s in range(2):
                    dve.wait_ge(gated.sem, i * 2 + (s + 1))
                    dve.tensor_tensor(K.hmid[:, bass.ds(i * 2 + s, 1), :].rearrange("p a t -> p (a t)"), conv[:, s, 0, :], conv[:, s, 1, :],
                                      ALU.mult).then_inc(done.sem, 1)

        @block.gpsimd
        def _(pool):
            pool.wait_ge(K.gates_out.sem, 16)
            spread(K, pool, 0, d["gate_rows"][0, KD:2 * KD, :].rearrange("k p -> (k p)"))
            for slot, name in ((1, "b_down"), (2, "ln1_g"), (3, "ln1_b")):
                spread(K, pool, slot, d["rows"][ROWS.index(name)])
            pool.wait_ge(K.rows_landed.sem, K.rows_landed.n)
            r = [K.row[:, i, :] for i in range(4)]
            link(pool, pool.tensor_tensor(r[1], r[0], r[1], ALU.mult), K.pool_step)
            link(pool, pool.tensor_scalar(r[3], r[3], ALPHA, 0.0, ALU.mult, ALU.add), K.pool_step)
            link(pool, pool.tensor_tensor(r[3], r[3], r[1], ALU.add), K.pool_step)
            link(pool, pool.tensor_scalar(r[2], r[2], ALPHA, 0.0, ALU.mult, ALU.add), K.pool_step)
            for t in range(NT):
                link(pool, pool.tensor_tensor(K.res[:, t, :], K.res[:, t, :], r[2], ALU.mult), K.pool_step)
                link(pool, pool.tensor_tensor(K.res[:, t, :], K.res[:, t, :], r[3], ALU.add), K.pool_step)
    K.memory.release("ffn_taps", "ffn_conv")


def phase_ffn_down(nc, K, ctx):
    d, sb, sig = K.dram, K.buffer, K.flag
    gated, z = sb("gated2", [P, D]), sb("z", [P, NT, D])
    mm, var, root, normed = sig("down_summed"), sig("var_2"), sig("root_2"), sig("normed_2")
    taken = sig("down_tile_used")
    squared, ms, root2, scaled = sig("x_squared"), sig("ms_2"), sig("root_rms"), sig("x_scaled")
    turned, moved = sig("turned_2"), sig("h_written_2")
    per = 4
    tiles = -(-NF // per)

    with nc.Block() as block:
        @block.tensor
        def _(pe):
            for n in range(tiles):
                w = take(K, pe).rearrange("p (k n) -> p k n", k=per)
                for t in range(NT):
                    for half in range(2):
                        for k in range(per * n, min(per * n + per, NF)):
                            last = pe.matmul(K.bank[2 * t + half], K.hmid[:, k, P * t:P * t + P], w[:, k % per, 512 * half:512 * half + 512],
                                             start=(k == 0), stop=(k == NF - 1))
                    if n == tiles - 1:
                        mm.by(last)
                if n < tiles - 1:
                    taken.by(last)
                free(K, mm if n == tiles - 1 else taken)
            turn_channels(K, pe, z, (scaled.sem, NT), turned, moved)

        @block.sync
        def _(sp):
            for n in range(2, tiles):
                stream(K, sp, d["w_down"][n][:, 0:min(per, NF - per * n) * D])
            stream(K, sp, d["w_in2"][0])
            stream(K, sp, d["w_in2"][1])

        @block.gpsimd
        def _(pool):
            spread(K, pool, 1, d["rows"][ROWS.index("ln2_g")])
            spread(K, pool, 2, d["rows"][ROWS.index("ln2_b")])

        @block.vector
        def _(dve):
            for t in range(NT):
                x = K.res[:, t, :]
                dve.wait_ge(mm.sem, t + 1)
                link(dve, dve.tensor_tensor(gated[:, :], K.psum[:, D * t:D * t + D], K.row[:, 0, :], ALU.mult), K.dve_step)
                link(dve, dve.tensor_tensor(x, x, gated[:, :], ALU.add), K.dve_step)
                norm_stats(K, dve, x, t, K.dve_step)
                link(dve, dve.tensor_scalar(K.rstd[:, t:t + 1], K.mv[:, t, 1:2], LN_EPS, None, ALU.add), var)
                dve.wait_ge(root.sem, t + 1)
                link(dve, dve.reciprocal(K.rstd[:, t:t + 1], K.rstd[:, t:t + 1]), K.dve_step)
                dve.wait_ge(K.rows_landed.sem, K.rows_landed.n)
                link(dve, dve.scalar_tensor_tensor(out=x, in0=x, scalar=K.mv[:, t, 0:1], in1=K.row[:, 1, :], op0=ALU.subtract, op1=ALU.mult), K.dve_step)
                link(dve, dve.scalar_tensor_tensor(out=x, in0=x, scalar=K.rstd[:, t:t + 1], in1=K.row[:, 2, :], op0=ALU.mult, op1=ALU.add), normed)
            for t in range(NT):
                dve.wait_ge(squared.sem, t + 1)
                link(dve, dve.tensor_scalar(K.rstd[:, t:t + 1], K.rstd[:, t:t + 1], 1.0 / D, RMS_EPS, ALU.mult, ALU.add), ms)
                dve.wait_ge(root2.sem, t + 1)
                link(dve, dve.reciprocal(K.rstd[:, t:t + 1], K.rstd[:, t:t + 1]), K.dve_step)
                scaled.by(dve.tensor_scalar(z[:, t, :], K.res[:, t, :], K.rstd[:, t:t + 1], None, ALU.mult))

        @block.scalar
        def _(act):
            for t in range(NT):
                act.wait_ge(var.sem, t + 1)
                root.by(act.activation(K.rstd[:, t:t + 1], K.rstd[:, t:t + 1], ACT.Sqrt))
            for t in range(NT):
                act.wait_ge(normed.sem, t + 1)
                squared.by(act.activation(z[:, t, :], K.res[:, t, :], ACT.Square, accum_out=K.rstd[:, t:t + 1]))
            for t in range(NT):
                act.wait_ge(ms.sem, t + 1)
                root2.by(act.activation(K.rstd[:, t:t + 1], K.rstd[:, t:t + 1], ACT.Sqrt))
            for k in range(KD):
                act.wait_ge(turned.sem, k + 1)
                moved.by(act.activation(K.h[:, k, :], K.bank[k % 4], ACT.Identity, bias=K.fold[:, 3, k:k + 1], scale=K.fold[:, 2, k:k + 1]))
    K.rows_expected = K.rows_landed.n
    K.memory.release("gated2", "z", "hmid")


ZQ, ZK, ZIQ, ZIK, ZR, ZKK, ZV, ZWA, ZG, ZIW = 0, 4, 8, 12, 13, 17, 21, 25, 26, 27
NZ = 28
TOE = 640


def phase_in2(nc, K, ctx):
    d, sb, sig = K.dram, K.buffer, K.flag
    K.z = sb("z2", [P, NZ, T])
    K.v2 = sb("v2", [P, NT, T])
    K.toe = sb("toe", [P, HEADS, T])
    relb, hot, line = sb("relb", [33, HEADS]), sb("hot", [33, TOE]), sb("toe_line", [HEADS, TOE])
    summed, act_out, dve_out = sig("z_summed"), sig("z_out_act"), sig("z_out_dve")
    v_mm, v_out = sig("v2_summed"), sig("v2_out")
    rel_ms, rel_in, toe_mm, toe_sb, toe_dma = sig("relb_set"), K.dma_signal("relb_landed"), sig("toe_summed"), sig("toe_copied"), K.dma_signal("toe_moved")
    K.toe_dma = toe_dma

    with nc.Block() as block:
        @block.tensor
        def _(pe):
            with pe.Fori(0, 3) as i:
                for s in range(2):
                    w = take_in_loop(K, pe, i, s).rearrange("p (k m) -> p k m", k=KD)
                    for b in range(4):
                        pe.wait_ge((act_out, dve_out)[b % 2].sem, i * 4 + (2 * s + b // 2 + 1))
                        for k in range(KD):
                            last = pe.matmul(K.bank[4 * s + b], w[:, k, P * b:P * b + P], K.h[:, k, :], start=(k == 0), stop=(k == KD - 1))
                        last.then_inc(summed.sem, 1)
            summed.n += 24
            K.ws_taken += 6
            for n in range(6):
                K.ws_freed.append((summed.sem, 4 * n + 4))
            w = take(K, pe).rearrange("p (k m) -> p k m", k=KD)
            for b in range(4):
                pe.wait_ge((act_out, dve_out)[b % 2].sem, 12 + b // 2 + 1)
                for k in range(KD):
                    last = pe.matmul(K.bank[b], w[:, k, P * b:P * b + P], K.h[:, k, :], start=(k == 0), stop=(k == KD - 1))
                summed.by(last)
            free(K, summed)
            w = take(K, pe).rearrange("p (k m) -> p k m", k=KD)
            for t in range(NT):
                pe.wait_ge((act_out, dve_out)[t % 2].sem, 14 + t // 2 + 1)
                for k in range(KD):
                    last = pe.matmul(K.bank[4 + t], K.h[:, k, P * t:P * t + P], w[:, k, :], start=(k == 0), stop=(k == KD - 1))
                v_mm.by(last)
            free(K, v_mm)
            pe.wait_ge(rel_in.sem, 32)
            pe.wait_ge(act_out.sem, 18)
            pe.wait_ge(dve_out.sem, 18)
            pe.matmul(K.bank[0][0:HEADS, 0:512], relb[:, :], hot[:, 0:512], start=True, stop=True)
            toe_mm.by(pe.matmul(K.bank[1][0:HEADS, 0:TOE - 512], relb[:, :], hot[:, 512:TOE], start=True, stop=True))

        @block.sync
        def _(sp):
            base = K.ws_issued
            with sp.Fori(0, 2) as i:
                for s in range(2):
                    sp.wait_ge(summed.sem, i * 8 + (4 * s + 4))
                    src = d["w_in2"][bass.ds(i * 2 + (2 + s), 1)].rearrange("a p n -> (a p) n")
                    sp.dma_start(K.ws[:, (base + s) % 2, :], src).then_inc(K.ws_landed[(base + s) % 2].sem, 16)
            for s in range(2):
                K.ws_landed[(base + s) % 2].n += 32
            K.ws_issued += 4
            stream(K, sp, d["w_in2"][6])
            stream(K, sp, d["w_v2"])

        @block.scalar
        def _(act):
            act.sem_inc(act_out.sem, 4)
            with act.Fori(0, 3) as i:
                for n in range(4):
                    act.wait_ge(summed.sem, i * 8 + (2 * n + 1))
                    act.activation(K.z[:, bass.ds(i * 8 + 2 * n, 1), :].rearrange("p a t -> p (a t)"), K.bank[2 * n], ACT.Copy).then_inc(act_out.sem, 1)
            for b in (0, 2):
                act.wait_ge(summed.sem, 24 + b + 1)
                act.activation(K.z[:, 24 + b, :], K.bank[b], ACT.Copy).then_inc(act_out.sem, 1)
            act_out.n = 18
            for t in range(NT):
                act.wait_ge(v_mm.sem, t + 1)
                v_out.by(act.activation(K.v2[:, t, :], K.bank[4 + t], ACT.Copy))
            act.wait_ge(toe_mm.sem, 1)
            act.activation(line[:, 0:512], K.bank[0][0:HEADS, :], ACT.Copy)
            toe_sb.by(act.activation(line[:, 512:TOE], K.bank[1][0:HEADS, 0:TOE - 512], ACT.Copy))

        @block.vector
        def _(dve):
            dve.sem_inc(dve_out.sem, 4)
            with dve.Fori(0, 3) as i:
                for n in range(4):
                    dve.wait_ge(summed.sem, i * 8 + (2 * n + 2))
                    dve.tensor_copy(K.z[:, bass.ds(i * 8 + (2 * n + 1), 1), :].rearrange("p a t -> p (a t)"), K.bank[2 * n + 1]).then_inc(dve_out.sem, 1)
            for b in (1, 3):
                dve.wait_ge(summed.sem, 24 + b + 1)
                dve.tensor_copy(K.z[:, 24 + b, :], K.bank[b]).then_inc(dve_out.sem, 1)
            dve_out.n = 18

        @block.gpsimd
        def _(pool):
            rel_ms.by(pool.memset(relb[:, :], -1.0e30))
            pool.wait_ge(rel_ms.sem, 1)
            rel_in.by(pool.dma_start(relb[0:32, :], d["rel_bias"]), 16)
            rel_in.by(pool.dma_start(hot[:, :], d["bucket_hot"]), 16)
            pool.wait_ge(toe_sb.sem, 1)
            toe_dma.by(pool.dma_start(d["toe_line"], line[:, :]), 16)
            pool.wait_ge(toe_dma.sem, 16)
    K.memory.release("relb", "hot", "toe_line")


TOPK, IDX_HEADS, IDX_DIM = min(256, T // 4), 16, 32
NEG, TAKEN = -3.0e38, -3.3e38
ATT_SCALE = 64 ** -0.5


def phase_sparse(nc, K, ctx):
    d, sb, sig = K.dram, K.buffer, K.flag
    K.att2 = sb("att2", [P, 4, T])
    qz = K.row[:, :, :].rearrange("p a n -> p (a n)").rearrange("p (h t) -> p h t", h=HEADS)
    iqz = K.ws[:, 0, 0:IDX_HEADS * P].rearrange("p (h t) -> p h t", h=IDX_HEADS)
    iw = sb("iw", [P, NT, P])
    dots = sb("dots", [P, 2, T])
    both = K.ws[:, 1, 0:2 * T].rearrange("p (a t) -> p a t", a=2)
    score, left = both[:, 0, :], both[:, 1, :]
    masked = [sb(f"masked{qt}", [P, P * (qt + 1)]) for qt in range(1, NT)]
    top = sb("top", [P, 8])
    logit, prob, probT = sb("logit", [P, 2, T]), dots, both
    nmax, rsum = sb("nmax2", [P, 32]), sb("rsum2", [P, 32])
    zeroed, qz_in, iqz_in, iw_mm, iw_out = sig("qz_zeroed"), sig("qz_ready"), sig("iqz_ready"), sig("iw_turned"), sig("iw_out")
    ix_mm, ix_act, ix_add, diag = sig("dots_summed"), sig("dots_relu"), sig("score_added"), sig("score_causal")
    cut = sig("top_taken")
    s_mm, mx, ex, pn = sig("scores_2"), sig("row_max_2"), sig("probs_2"), sig("probs_normed")
    t_pe, t_sb, pv, o_sb = sig("probs_turned_2"), sig("probsT_out_2"), sig("pv_summed_2"), sig("att_out_2")
    UNITS = NT * HEADS
    keys = lambda qt: P * (qt + 1)

    with nc.Block() as block:
        @block.tensor
        def _(pe):
            for t in range(NT):
                last = pe.transpose(K.bank[7][:, P * t:P * t + P], K.z[:, ZIW, P * t:P * t + P], K.ident[:, :])
            iw_mm.by(last)
            n = 0
            for qt in range(1, NT):
                pe.wait_ge(iqz_in.sem, qt)
                for h in range(IDX_HEADS):
                    if n >= 2:
                        pe.wait_ge(ix_act.sem, n - 1)
                    ix_mm.by(pe.matmul(K.bank[n % 2][:, 0:keys(qt)], iqz[:, h, :], K.z[:, ZIK, 0:keys(qt)], start=True, stop=True))
                    n += 1
            pe.wait_ge(qz_in.sem, 1)
            pe.wait_ge(iw_out.sem, 1)

            def scores(n):
                qt, h = divmod(n, HEADS)
                if n >= 2:
                    pe.wait_ge(mx.sem, n - 1)
                s_mm.by(pe.matmul(K.bank[2 + n % 2][:, 0:keys(qt)], qz[:, h, P * qt:P * qt + P], K.z[:, ZK + h // 2, 0:keys(qt)], start=True, stop=True))

            def turn(n):
                qt = n // HEADS
                pe.wait_ge(pn.sem, n + 1)
                if n >= 2:
                    pe.wait_ge(t_sb.sem, n - 1)
                for k in range(qt + 1):
                    last = pe.transpose(K.bank[4 + n % 2][:, P * k:P * k + P], prob[:, n % 2, P * k:P * k + P], K.ident[:, :])
                t_pe.by(last)

            def weigh(n):
                qt, h = divmod(n, HEADS)
                pe.wait_ge(t_sb.sem, n + 1)
                if h == 0 and qt >= 2:
                    pe.wait_ge(o_sb.sem, qt - 1)
                a = 64 * (h % 2)
                for k in range(qt + 1):
                    last = pe.matmul(K.bank[6 + qt % 2][a:a + 64, P * (h // 2):P * (h // 2) + P], K.v2[:, k, 64 * h:64 * h + 64],
                                     probT[:, n % 2, P * k:P * k + P], start=(k == 0), stop=(k == qt))
                pv.by(last)

            for n in range(UNITS + 3):
                if n < UNITS:
                    scores(n)
                if 2 <= n <= UNITS + 1:
                    turn(n - 2)
                if n >= 3:
                    weigh(n - 3)

        @block.scalar
        def _(act):
            act.wait_ge(iw_mm.sem, 1)
            iw_out.by(act.activation(iw[:, :, :].rearrange("p t h -> p (t h)"), K.bank[7], ACT.Copy, scale=(IDX_HEADS * IDX_DIM) ** -0.5))
            n = 0
            for qt in range(1, NT):
                for h in range(IDX_HEADS):
                    act.wait_ge(ix_mm.sem, n + 1)
                    if n >= 2:
                        act.wait_ge(ix_add.sem, n - 1)
                    ix_act.by(act.activation(dots[:, n % 2, 0:keys(qt)], K.bank[n % 2][:, 0:keys(qt)], ACT.Relu))
                    n += 1

            def exps(n):
                w = keys(n // HEADS)
                act.wait_ge(mx.sem, n + 1)
                if n >= 2:
                    act.wait_ge(t_pe.sem, n - 1)
                ex.by(act.activation(prob[:, n % 2, 0:w], logit[:, n % 2, 0:w], ACT.Exp, bias=nmax[:, n:n + 1], accum_out=rsum[:, n:n + 1]))

            def turned(n):
                w = keys(n // HEADS)
                act.wait_ge(t_pe.sem, n + 1)
                if n >= 2:
                    act.wait_ge(pv.sem, n - 1)
                t_sb.by(act.activation(probT[:, n % 2, 0:w], K.bank[4 + n % 2][:, 0:w], ACT.Copy))

            def output(qt):
                act.wait_ge(pv.sem, HEADS * (qt + 1))
                o_sb.by(act.activation(K.att2[:, :, P * qt:P * qt + P], K.bank[6 + qt % 2].rearrange("p (c q) -> p c q", c=4), ACT.Copy))

            for n in range(UNITS + 2):
                if n < UNITS:
                    exps(n)
                if n >= 2:
                    turned(n - 2)
                if n >= HEADS + 2 and (n - 2) % HEADS == 2:
                    output((n - 2) // HEADS - 1)
            output(NT - 1)

        @block.gpsimd
        def _(pool):
            link(pool, pool.memset(iqz[:, :, :], 0.0), zeroed)
            link(pool, pool.memset(qz, 0.0), zeroed)
            for qt in range(1, NT):
                if qt > 1:
                    pool.wait_ge(ix_mm.sem, IDX_HEADS * (qt - 1))
                for h in range(IDX_HEADS):
                    a = IDX_DIM * (h % 4)
                    link(pool, pool.tensor_copy(iqz[a:a + IDX_DIM, h, :], K.z[a:a + IDX_DIM, ZIQ + h // 4, P * qt:P * qt + P]), K.pool_step if h < IDX_HEADS - 1 else iqz_in)
                if qt == 1:
                    K.toe_dma.by(pool.dma_start(d["toe_wide"][0:P * HEADS * TOE].rearrange("(p n) -> p n", p=P),
                                              d["toe_line"].rearrange("h t -> (h t)").partition_broadcast(P)), 16)
                    for h in range(HEADS):
                        a = 64 * (h % 2)
                        link(pool, pool.tensor_copy(qz[a:a + 64, h, :], K.z[a:a + 64, ZQ + h // 2, :]), K.pool_step if h < HEADS - 1 else qz_in)
                pool.wait_ge(ix_add.sem, IDX_HEADS * qt)
                b = score[:, P * qt:P * qt + P]
                diag.by(pool.affine_select(out=b, in_=b, compare_op=ALU.is_ge, fill=NEG, base=0, pattern=[[-1, P]], channel_multiplier=1))
                if qt == 1:
                    pool.wait_ge(K.toe_dma.sem, 32)
                    src = d["toe_wide"][P - 1:P - 1 + P * (HEADS * TOE - 1)].rearrange("(p n) -> p n", p=P)
                    for h in range(HEADS):
                        K.toe_dma.by(pool.dma_start(K.toe[:, h, :], src[:, TOE * h:TOE * h + T]), 16)

        @block.vector
        def _(dve):
            dve.wait_ge(iw_out.sem, 1)
            n = 0
            for qt in range(1, NT):
                w = keys(qt)
                for h in range(IDX_HEADS):
                    dve.wait_ge(ix_act.sem, n + 1)
                    if h == 0:
                        ix_add.by(dve.tensor_scalar(score[:, 0:w], dots[:, n % 2, 0:w], iw[:, qt, 0:1], None, ALU.mult))
                    else:
                        dve.wait_ge(ix_add.sem, n)
                        ix_add.by(dve.scalar_tensor_tensor(out=score[:, 0:w], in0=dots[:, n % 2, 0:w], scalar=iw[:, qt, h:h + 1],
                                                           in1=score[:, 0:w], op0=ALU.mult, op1=ALU.add))
                    n += 1
                dve.wait_ge(diag.sem, qt)
                for r in range(TOPK // 8):
                    src = (left if r else score)[:, 0:w]
                    link(dve, dve.max(top[:, :], src), K.dve_step)
                    link(dve, dve.match_replace(left[:, 0:w], top[:, :], src, TAKEN), K.dve_step)
                m = masked[qt - 1]
                link(dve, dve.tensor_tensor(m[:, :], left[:, 0:w], score[:, 0:w], ALU.is_equal), K.dve_step)
                link(dve, dve.tensor_scalar(m[:, :], m[:, :], -1.0e30, None, ALU.mult), cut)

            dve.wait_ge(K.toe_dma.sem, 16 * (2 + HEADS))

            def logits(n):
                qt, h = divmod(n, HEADS)
                w = keys(qt)
                x = logit[:, n % 2, 0:w]
                dve.wait_ge(s_mm.sem, n + 1)
                link(dve, dve.scalar_tensor_tensor(out=x, in0=K.bank[2 + n % 2][:, 0:w], scalar=ATT_SCALE, in1=K.toe[:, h, T - w:T],
                                                   op0=ALU.mult, op1=ALU.add), K.dve_step)
                if qt:
                    link(dve, dve.tensor_tensor(x, x, masked[qt - 1][:, :], ALU.add), K.dve_step)
                mx.by(dve.tensor_reduce(nmax[:, n:n + 1], x, AX.X, ALU.max, negate=True))

            def norm(n):
                w = keys(n // HEADS)
                dve.wait_ge(ex.sem, n + 1)
                link(dve, dve.reciprocal(rsum[:, n:n + 1], rsum[:, n:n + 1]), K.dve_step)
                pn.by(dve.tensor_scalar(prob[:, n % 2, 0:w], prob[:, n % 2, 0:w], rsum[:, n:n + 1], None, ALU.mult))

            for n in range(UNITS + 1):
                if n < UNITS:
                    logits(n)
                if n:
                    norm(n - 1)
    K.memory.release("iw", "dots", "masked1", "masked2", "masked3", "top", "logit", "nmax2", "rsum2", "v2", "toe")


C = P
NCH = T // C
SUB = 16
DECAY = float(np.exp(-0.5))
M_D, M_F, M_DT, M_S, M_I, M_BLOCK = range(6)


def phase_recur(nc, K, ctx):
    d, sb, sig = K.dram, K.buffer, K.flag
    row = K.row[:, :, :].rearrange("p a n -> p (a n)")
    ar = sb("ar", [P, 4, 2, T])
    bk = sb("bk", [P, 4, 2, T])
    low = K.z[:, 0:13, :].rearrange("p a t -> p (a t)")
    masks = sb("masks", [P, 6, P])
    ups = K.z[:, 8:11, :]
    sg, av, cs, t1, t2, pe_ = (low[:, T * i:T * i + T] for i in range(6))
    starts, xw = low[:, T * 6:T * 7], low[:, T * 7:T * 8]
    small = sb("small_r", [P, 18])
    pc = sb("pc", [P, 4, NCH])
    zr, zk, zv = K.z[:, ZR:ZR + 4, :], K.z[:, ZKK:ZKK + 4, :], K.z[:, ZV:ZV + 4, :]
    s = sig
    masks_in, shifted, inv_mu = s("masks_landed"), s("shifted"), s("inv_mu")
    tanh, lo_mm, lo_a, lo_w = s("tanh_done"), s("lora_summed"), s("lora_a_out"), s("lora_w_out")
    gsig, g_mm, g_out = s("gate_sigmoid"), s("gate_summed"), s("gate_out")
    cumul, cmin, expd = s("decay_cumulated"), s("decay_before"), s("decay_exps")
    ksq, ss_mm, nrm, made = s("k_squared"), s("k_squares_summed"), s("k_norm"), s("chunk_operands")
    bo_in, bo_mm, filled = s("bonus_in"), s("bonus_summed"), s("expert_out_filled")

    with nc.Block() as block:
        @block.sync
        def _(sp):
            masks_in.by(sp.dma_start(masks[:, :, :], d["masks"]), 16)
            masks_in.by(sp.dma_start(ups[:, :, :], d["ups"]), 16)
            for n in range(T * TOP // BLOCK, BLOCKS, NT):
                filled.by(sp.dma_start(d["expert_out"][n:n + NT].rearrange("b p n -> p b n"), K.res[:, :, :]), 16)
            sp.wait_ge(filled.sem, filled.n)

        @block.tensor
        def _(pe):
            pe.wait_ge(masks_in.sem, 32)
            for c in range(4):
                if c == 0:
                    pe.wait_ge(tanh.sem, 2)
                else:
                    pe.wait_ge(lo_w.sem, c)
                    pe.wait_ge(lo_a.sem, c)
                pe.matmul(K.bank[0], ups[:, 0, P * c:P * c + P], xw, start=True, stop=True)
                lo_mm.by(pe.matmul(K.bank[1], ups[:, 1, P * c:P * c + P], xw, start=True, stop=True))
                if c == 0:
                    pe.wait_ge(gsig.sem, 1)
                else:
                    pe.wait_ge(g_out.sem, c)
                g_mm.by(pe.matmul(K.bank[2], ups[:, 2, P * c:P * c + P], K.z[:, ZG, :], start=True, stop=True))
                pe.wait_ge(ksq.sem, c + 1)
                ss_mm.by(pe.matmul(K.bank[3], masks[:, M_BLOCK, :], t1, start=True, stop=True))
                pe.wait_ge(bo_in.sem, c + 1)
                bo_mm.by(pe.matmul(K.bank[4], masks[:, M_BLOCK, :], t1, start=True, stop=True))

        @block.scalar
        def _(act):
            act.wait_ge(shifted.sem, 14)
            act.activation(xw[0:64, :], K.z[0:64, ZWA, :], ACT.Tanh).then_inc(tanh.sem, 1)
            tanh.by(act.activation(xw[64:P, :], K.z[64:P, ZWA, :], ACT.Copy))
            gsig.by(act.activation(K.z[:, ZG, :], K.z[:, ZG, :], ACT.Sigmoid))
            for c in range(4):
                act.wait_ge(lo_mm.sem, c + 1)
                if c:
                    act.wait_ge(made.sem, c)
                lo_w.by(act.activation(sg, K.bank[0], ACT.Sigmoid, bias=col(K, "decay_w0_2", c)))
                lo_a.by(act.activation(av, K.bank[1], ACT.Sigmoid, bias=col(K, "iclr_a0_2", c)))
                ksq.by(act.activation(t1, zk[:, c, :], ACT.Square, scale=col(K, "k_k_2", c)))
                act.wait_ge(ss_mm.sem, c + 1)
                nrm.by(act.activation(t2, K.bank[3], ACT.Sqrt))
                act.wait_ge(cumul.sem, c + 1)
                act.activation(ar[:, c, 1, :], cs, ACT.Exp, scale=-DECAY).then_inc(expd.sem, 1)
                act.activation(bk[:, c, 1, :], cs, ACT.Exp, scale=DECAY).then_inc(expd.sem, 1)
                act.wait_ge(cmin.sem, c + 1)
                act.activation(ar[:, c, 0, :], pe_, ACT.Exp, scale=-DECAY).then_inc(expd.sem, 1)
                act.wait_ge(g_mm.sem, c + 1)
                act.wait_ge(made.sem, c + 1)
                g_out.by(act.activation(zk[:, c, :], K.bank[2], ACT.Copy))

        @block.gpsimd
        def _(pool):
            pass

        @block.vector
        def _(dve):
            link(dve, dve.tensor_scalar(small[:, 0:14], col(K, "tshift_mu_2", 0, 14), -1.0, 1.0, ALU.mult, ALU.add), inv_mu)
            link(dve, dve.tensor_scalar(small[:, 14:18], col(K, "k_a_2", 0, 4), -1.0, 1.0, ALU.mult, ALU.add), inv_mu)
            for n in [12, 13] + list(range(12)):
                x = K.z[:, ZR + n, :]
                t = (t1, t2)[n % 2]
                link(dve, dve.tensor_tensor(t[:, 0:T - 1], x[:, 0:T - 1], x[:, 1:T], ALU.subtract), K.dve_step)
                dve.tensor_scalar(x[:, 0:1], x[:, 0:1], small[:, n:n + 1], None, ALU.mult).then_inc(K.dve_step.sem, 1)
                K.dve_step.n += 1
                shifted.by(dve.scalar_tensor_tensor(out=x[:, 1:T], in0=t[:, 0:T - 1], scalar=col(K, "tshift_mu_2", n), in1=x[:, 1:T],
                                                    op0=ALU.mult, op1=ALU.add))
            dve.wait_ge(K.dve_step.sem, K.dve_step.n)
            dve.wait_ge(shifted.sem, 14)
            link(dve, dve.memset(starts, 1.0), K.dve_step)
            link(dve, dve.memset(starts.rearrange("p (c t) -> p c t", c=NCH)[:, :, 0:1], 0.0), K.dve_step)
            for c in range(4):
                dve.wait_ge(lo_w.sem, c + 1)
                link(dve, dve.tensor_tensor_scan(cs, starts, sg, 0.0, ALU.mult, ALU.add), cumul)
                link(dve, dve.tensor_tensor(pe_, cs, sg, ALU.subtract), cmin)
                dve.wait_ge(nrm.sem, c + 1)
                link(dve, dve.tensor_scalar(t2, t2, 1e-12, None, ALU.max), K.dve_step)
                link(dve, dve.reciprocal(t2, t2), K.dve_step)
                link(dve, dve.scalar_tensor_tensor(out=t2, in0=zk[:, c, :], scalar=col(K, "k_k_2", c), in1=t2, op0=ALU.mult, op1=ALU.mult), K.dve_step)
                dve.wait_ge(lo_a.sem, c + 1)
                link(dve, dve.tensor_scalar(t1, av, col(K, "k_a_2", c), small[:, 14 + c:15 + c], ALU.mult, ALU.add), K.dve_step)
                dve.wait_ge(ss_mm.sem, c + 1)
                link(dve, dve.tensor_tensor(zk[:, c, :], zk[:, c, :], t1, ALU.mult), K.dve_step)
                link(dve, dve.scalar_tensor_tensor(out=t1, in0=zr[:, c, :], scalar=col(K, "r_k_2", c), in1=zk[:, c, :], op0=ALU.mult, op1=ALU.mult), bo_in)
                dve.wait_ge(expd.sem, 3 * c + 3)
                link(dve, dve.tensor_copy(pc[:, c, :], ar[:, c, 1, :].rearrange("p (c t) -> p c t", c=NCH)[:, :, C - 1]), K.dve_step)
                link(dve, dve.scalar_tensor_tensor(out=ar[:, c, 0, :], in0=ar[:, c, 0, :], scalar=-1.0, in1=t2, op0=ALU.mult, op1=ALU.mult), K.dve_step)
                link(dve, dve.tensor_tensor(ar[:, c, 1, :], ar[:, c, 1, :], zr[:, c, :], ALU.mult), K.dve_step)
                link(dve, dve.tensor_tensor(t2, t2, av, ALU.mult), K.dve_step)
                link(dve, dve.tensor_tensor(bk[:, c, 0, :], t2, bk[:, c, 1, :], ALU.mult), K.dve_step)
                link(dve, dve.tensor_tensor(bk[:, c, 1, :], bk[:, c, 1, :], zk[:, c, :], ALU.mult), K.dve_step)
                dve.wait_ge(bo_mm.sem, c + 1)
                link(dve, dve.tensor_tensor(zr[:, c, :], K.bank[4], zv[:, c, :], ALU.mult), made)
    K.memory.release("small_r")

    inv = {name: low[:, 1024 * i:1024 * i + 1024].rearrange("p (g n) -> p g n", g=2) for i, name in enumerate(("D", "D'", "F", "D2", "D2'", "D4"))}
    inv["D4'"] = row[:, 0:1024].rearrange("p (g n) -> p g n", g=2)
    inv["D8'"] = row[:, 1024:2048].rearrange("p (g n) -> p g n", g=2)
    tt = row[:, 2048:3072].rearrange("p (h t) -> p h t", h=HEADS)
    inv["Q"] = row[:, 2048:3072].rearrange("p (g n) -> p g n", g=2)
    gb = row[:, 3072:4096].rearrange("p (h t) -> p h t", h=HEADS)
    mh = K.ws[:, 0, 0:2048].rearrange("p (h m t) -> p h m t", h=HEADS, m=2)
    bkz = K.ws[:, 0, 2048:4096].rearrange("p (h m t) -> p h m t", h=HEADS, m=2)
    xu = K.ws[:, 1, 0:1024].rearrange("p (a t) -> p a t", a=2)
    state = K.ws[:, 1, 1024:1536].rearrange("p (q n) -> p q n", q=4)
    tm = K.z[:, ZWA:ZWA + 3, :]
    y = K.y = lambda c: zv[:, :, C * c:C * c + C]
    steps = [
        ("D'", "D", "D2", False), ("D", "D'", "D2'", False), ("D2'", "D2", "D4", False), ("D2", "D2'", "D4'", False), ("D4", "D4'", "D8'", False),
        ("D2'", "Q", "Q", True), ("D4'", "Q", "Q", True), ("D8'", "Q", "Q", True), ("Q", None, "D4'", False),
        ("D4'", "F", "D", False), ("F", "D4'", "D'", False), ("D'", "D", "D2", False), ("D", "D'", "D2'", False), ("D2", "D2'", "D4", False),
        ("D'", "Q", "Q", True), ("D2'", "Q", "Q", True), ("D4", "Q", "Q", True)]
    zero, bz_in = s("state_zeroed"), s("bkz_ready")
    pr_mm, pr_out, tr_pe, tr_out = s("products"), s("products_masked"), s("tm_turned"), s("tm_out")
    st_mm, st_act, st_dve = s("inverse_step"), s("inverse_copied"), s("inverse_added")
    x_mm, x_out, u_mm, u_out, y_mm, y_out, s_mm, s_out = (s(n) for n in ("x_mm", "x_out", "u_mm", "u_out", "y_mm", "y_out", "state_mm", "state_out"))
    adds = [i for i, x in enumerate(steps) if x[3]]
    copies = [i for i, x in enumerate(steps) if not x[3]]

    def after_step(engine, c, i, g):
        if steps[i][3]:
            engine.wait_ge(st_dve.sem, 2 * (len(adds) * c + adds.index(i)) + g + 1)
        else:
            engine.wait_ge(st_act.sem, 2 * (len(copies) * c + copies.index(i)) + g + 1)

    def maker(name, i):
        return max((j for j in range(i) if steps[j][2] == name), default=None)

    pair = lambda banks: K.psum[:, 512 * banks:512 * banks + 1024].rearrange("p (q h n) -> p q h n", q=4, h=2)
    halves = lambda ap: ap.rearrange("p (q h n) -> p q h n", q=4, h=2)

    with nc.Block() as block:
        @block.tensor
        def _(pe):
            for c in range(NCH):
                now = slice(C * c, C * c + C)
                if c:
                    pe.wait_ge(s_out.sem, c)
                    pe.wait_ge(y_out.sem, 2 * c)
                for j in range(3):
                    for q in range(4):
                        src = zv[:, q, now] if j == 2 else bk[:, q, j, now]
                        last = pe.transpose(K.bank[j][:, P * q:P * q + P], src, K.ident[:, :])
                    tr_pe.by(last)
                pe.wait_ge(bz_in.sem, c + 1)
                for j in range(2):
                    for q in range(4):
                        bank = K.bank[(3 + 4 * j + q) % 8]
                        if 4 * j + q >= 5:
                            pe.wait_ge(tr_out.sem, 3 * c + 4 * j + q - 4)
                        for h in range(2):
                            last = pe.matmul(bank[:, 256 * h:256 * h + 256], bkz[:, 2 * q + h, j, :], ar[:, q, :, now], start=True, stop=True)
                        pr_mm.by(last)
                for g in range(2):
                    pe.wait_ge(pr_out.sem, 10 * c + 2 * g + 2)
                    for h in range(4):
                        q = 2 * g + h // 2
                        last = pe.matmul(K.bank[3 + 2 * g][:, C * h:C * h + C], ar[:, q, 0, now], bkz[:, 4 * g + h, 0, :], start=True, stop=True)
                    pr_mm.by(last)
                pe.wait_ge(pr_out.sem, 10 * c + 10)
                for i, (left, right, _, _) in enumerate(steps):
                    for g in range(2):
                        if i >= 4:
                            after_step(pe, c, i - 4, g)
                        for name in (left, right):
                            if name is not None and maker(name, i) is not None:
                                after_step(pe, c, maker(name, i), g)
                        for h in range(4):
                            out, a = K.bank[(2 * i + g) % 8][:, C * h:C * h + C], inv[left][:, g, C * h:C * h + C]
                            if right is None:
                                last = pe.transpose(out, a, K.ident[:, :])
                            else:
                                last = pe.matmul(out, a, inv[right][:, g, C * h:C * h + C], start=True, stop=True)
                        st_mm.by(last)
                for g in range(2):
                    for i in range(len(steps) - 4, len(steps)):
                        after_step(pe, c, i, g)
                pe.wait_ge(zero.sem, 2)
                for h in range(HEADS):
                    q = h // 2
                    out = K.psum[:, P * h:P * h + P]
                    pe.matmul(out, mh[:, h, 0, :], tm[:, 2, P * q:P * q + P], start=True, stop=False)
                    last = pe.matmul(out, ar[:, q, 0, now], state[:, q, :], start=False, stop=True)
                x_mm.by(last)
                for h in range(HEADS):
                    q = h // 2
                    out = K.psum[:, 1024 + P * h:1024 + P * h + P]
                    pe.matmul(out, mh[:, h, 1, :], tm[:, 2, P * q:P * q + P], start=True, stop=False)
                    pe.matmul(out, ar[:, q, 1, now], state[:, q, :], start=False, stop=True)
                    if h == 0:
                        pe.wait_ge(x_out.sem, 2 * c + 2)
                    u = K.psum[:, 2048 + P * h:2048 + P * h + P]
                    last = pe.matmul(u, tt[:, h, :], xu[:, 0, P * q:P * q + P], start=True, stop=True)
                    if h == HEADS - 1:
                        u_mm.by(last)
                pe.wait_ge(u_out.sem, 2 * c + 2)
                for h in range(HEADS):
                    q = h // 2
                    last = pe.matmul(K.psum[:, 3072 + P * h:3072 + P * h + P], gb[:, h, :], xu[:, 1, P * q:P * q + P], start=True, stop=True)
                y_mm.by(last)
                for q in range(4):
                    out = K.bank[0][:, P * q:P * q + P]
                    pe.matmul(out, tm[:, 0, P * q:P * q + P], xu[:, 1, P * q:P * q + P], start=True, stop=False)
                    last = pe.matmul(out, tm[:, 1, P * q:P * q + P], tm[:, 2, P * q:P * q + P], start=False, stop=True)
                s_mm.by(last)

        @block.scalar
        def _(act):
            for c in range(NCH):
                for j in range(3):
                    act.wait_ge(tr_pe.sem, 3 * c + j + 1)
                    tr_out.by(act.activation(tm[:, j, :], K.bank[j], ACT.Copy))
                for n, i in enumerate(copies):
                    for g in range(2):
                        act.wait_ge(st_mm.sem, 2 * (len(steps) * c + i) + g + 1)
                        st_act.by(act.activation(inv[steps[i][2]][:, g, :], K.bank[(2 * i + g) % 8], ACT.Copy))

        @block.gpsimd
        def _(pool):
            link(pool, pool.memset(bkz[:, :, :, :], 0.0), zero)
            link(pool, pool.memset(state[:, :, :], 0.0), zero)
            for c in range(NCH):
                if c:
                    pool.wait_ge(pr_mm.sem, 10 * c)
                for h in range(HEADS):
                    a = 64 * (h % 2)
                    link(pool, pool.tensor_copy(bkz[a:a + 64, h, :, :], bk[a:a + 64, h // 2, :, C * c:C * c + C]), K.pool_step if h < HEADS - 1 else bz_in)

        @block.vector
        def _(dve):
            spread_mask = lambda m, n: masks[:, m, :].unsqueeze(1).to_broadcast([P, n, P])
            for c in range(NCH):
                for n in range(8):
                    j, q = divmod(n, 4)
                    dve.wait_ge(pr_mm.sem, 10 * c + n + 1)
                    x = K.bank[(3 + n) % 8].rearrange("p (h v t) -> p h v t", h=2, v=2)
                    if j == 0:
                        to = {m: inv[m].rearrange("p g (h t) -> p (g h) t", h=4)[:, 2 * q:2 * q + 2, :] for m in ("D", "F")}
                        dve.tensor_tensor(to["D"], x[:, :, 0, :], spread_mask(M_D, 2), ALU.mult).then_inc(K.dve_step.sem, 1)
                        dve.tensor_tensor(to["F"], x[:, :, 0, :], spread_mask(M_F, 2), ALU.mult).then_inc(K.dve_step.sem, 1)
                        K.dve_step.n += 2
                        pr_out.by(dve.tensor_tensor(gb[:, 2 * q:2 * q + 2, :], x[:, :, 1, :], spread_mask(M_I, 2), ALU.mult))
                    else:
                        m = masks[:, M_S:M_S + 2, :].unsqueeze(1).to_broadcast([P, 2, 2, P])
                        pr_out.by(dve.tensor_tensor(mh[:, 2 * q:2 * q + 2, :, :], x, m, ALU.mult))
                for g in range(2):
                    dve.wait_ge(pr_mm.sem, 10 * c + 9 + g)
                    dve.tensor_tensor(inv["D'"][:, g, :].rearrange("p (h t) -> p h t", h=4),
                                      K.bank[3 + 2 * g].rearrange("p (h t) -> p h t", h=4), spread_mask(M_DT, 4), ALU.mult).then_inc(K.dve_step.sem, 1)
                    K.dve_step.n += 1
                    dve.wait_ge(K.dve_step.sem, K.dve_step.n)
                    pr_out.by(dve.tensor_tensor(inv["Q"][:, g, :].rearrange("p (h t) -> p h t", h=4), inv["D"][:, g, :].rearrange("p (h t) -> p h t", h=4),
                                                K.ident[:, :].unsqueeze(1).to_broadcast([P, 4, P]), ALU.add))
                for i in adds:
                    for g in range(2):
                        dve.wait_ge(st_mm.sem, 2 * (len(steps) * c + i) + g + 1)
                        q = inv["Q"][:, g, :]
                        if maker("Q", i) is not None:
                            after_step(dve, c, maker("Q", i), g)
                        else:
                            dve.wait_ge(pr_out.sem, 10 * c + 10)
                        st_dve.by(dve.tensor_tensor(q, q, K.bank[(2 * i + g) % 8], ALU.add))
                for what, (mm, at, to, out) in enumerate(((x_mm, 0, xu[:, 0, :], x_out), (u_mm, 4, xu[:, 1, :], u_out), (y_mm, 6, y(c), y_out))):
                    dve.wait_ge(mm.sem, c + 1)
                    src = pair(at)
                    for h in range(2):
                        to_h, src_h = (to[:, :, 64 * h:64 * h + 64] if what == 2 else halves(to)[:, :, h, :]), src[:, :, h, 64 * h:64 * h + 64]
                        if what == 2:
                            link(dve, dve.tensor_copy(to_h, src_h), K.dve_step)
                            out.by(dve.tensor_tensor(to_h, to_h, pair(2)[:, :, h, 64 * h:64 * h + 64], ALU.add))
                        else:
                            out.by(dve.tensor_copy(to_h, src_h))
                dve.wait_ge(s_mm.sem, c + 1)
                new = K.bank[0].rearrange("p (q n) -> p q n", q=4)
                for h in range(2):
                    a = slice(64 * h, 64 * h + 64)
                    link(dve, dve.tensor_tensor(state[a, :, a], state[a, :, a], new[a, :, a], ALU.add), K.dve_step)
                    last = dve.tensor_tensor(state[a, :, a], state[a, :, a], pc[a, :, c].unsqueeze(2).to_broadcast([64, 4, 64]), ALU.mult)
                    link(dve, last, s_out if h else K.dve_step)
    K.memory.release("masks", "ar", "bk", "pc")


def phase_branches(nc, K, ctx):
    d, sb, sig = K.dram, K.buffer, K.flag
    sga = K.row[:, :, :].rearrange("p a n -> p (a n)").rearrange("p (k t) -> p k t", k=KD)
    sgr, rw = K.z[:, 0:8, :], K.z[:, 8:12, :]
    sq, gated = sb("sq_gn", [P, 4, T]), sb("gated3", [P, D])
    K.h2 = sb("h2", [P, NT, D])
    mean, rstd = sb("gn_mean", [P, 32]), sb("gn_rstd", [P, 32])
    bonus, gate, y = K.z[:, ZR:ZR + 4, :], K.z[:, ZKK:ZKK + 4, :], K.z[:, ZV:ZV + 4, :]
    groups = lambda ap: ap.rearrange("p q (g n) -> p (q g) n", n=64)
    spread_group = lambda ap: ap.unsqueeze(2).to_broadcast([P, 32, 64])
    summed, act_out, dve_out = sig("branch_summed"), sig("branch_out_act"), sig("branch_out_dve")
    gvar, groot, gnormed = sig("gn_var"), sig("gn_root"), sig("gn_normed")
    rw_ready, mixed, mm = sig("rw_ready"), sig("mixed"), sig("w_out_summed")
    x2, squared, ms, root, scaled = sig("x2_ready"), sig("x2_squared"), sig("ms_h2"), sig("root_h2"), sig("h2_ready")
    turned, moved, h2_out = sig("turned_h2"), sig("h2_channels"), K.flag("h2_in_dram")
    units = ([("ga", m) for m in range(KD)] + [("at", m) for m in range(KD)] + [("gr", m) for m in range(4)] +
             [("turn", q) for q in range(4)] + [("gr", m) for m in range(4, KD)] + [("rw", m) for m in range(KD)])
    by_dve = [kind in ("at", "rw") for kind, _ in units]

    def read(engine, n):
        mine = [i for i in range(n + 1) if by_dve[i] == by_dve[n]]
        engine.wait_ge((dve_out if by_dve[n] else act_out).sem, len(mine))

    with nc.Block() as block:
        @block.tensor
        def _(pe):
            w = None
            for n, (kind, m) in enumerate(units):
                per = 4 if kind in ("ga", "gr") else KD
                if kind != "turn" and m % per == 0:
                    w = take(K, pe).rearrange("p (k m) -> p k m", k=KD if per == 4 else 4)
                if n >= 8:
                    read(pe, n - 8)
                if kind == "turn":
                    pe.wait_ge(gnormed.sem, 1)
                    for t in range(NT):
                        last = pe.transpose(K.bank[n % 8][:, P * t:P * t + P], y[:, m, P * t:P * t + P], K.ident[:, :])
                else:
                    src = K.h if per == 4 else K.att2
                    if kind == "rw":
                        src = rw
                        pe.wait_ge(rw_ready.sem, 4)
                    inner = KD if per == 4 else 4
                    for k in range(inner):
                        at = P * (m % per)
                        last = pe.matmul(K.bank[n % 8], w[:, k, at:at + P], src[:, k, :], start=(k == 0), stop=(k == inner - 1))
                summed.by(last)
                if kind != "turn" and m % per == per - 1:
                    free(K, summed)
            pe.wait_ge(mixed.sem, KD)
            for n in range(len(units) - 16, len(units)):
                read(pe, n)
            project_tokens(K, pe, sga, 2, 4, mm)
            pe.wait_ge(x2.sem, NT)
            turn_channels(K, pe, K.h2, (scaled.sem, NT), turned, moved)

        @block.sync
        def _(sp):
            for src in (d["w_gates"][0], d["w_gates"][1], d["w_attn_br"], d["w_gates"][2], d["w_gates"][3], d["w_rwkv_br"], d["w_out"][0], d["w_out"][1]):
                stream(K, sp, src)
            for t in range(NT):
                sp.wait_ge(scaled.sem, t + 1)
                h2_out.by(sp.dma_start(d["h2"][P * t:P * t + P, :], K.h2[:, t, :]), 16)
            sp.wait_ge(h2_out.sem, h2_out.n)

        @block.scalar
        def _(act):
            for n, (kind, m) in enumerate(units):
                if kind == "at" and m == 0:
                    act.wait_ge(gvar.sem, 1)
                    groot.by(act.activation(rstd[:, :], rstd[:, :], ACT.Sqrt))
                if by_dve[n]:
                    continue
                act.wait_ge(summed.sem, n + 1)
                if kind == "turn":
                    act_out.by(act.activation(rw[:, m, :], K.bank[n % 8], ACT.Identity, bias=col(K, "lnx_b_2", m), scale=col(K, "lnx_g_2", m)))
                else:
                    act_out.by(act.activation((sga if kind == "ga" else sgr)[:, m, :], K.bank[n % 8], ACT.Sigmoid))
            for t in range(NT):
                act.wait_ge(x2.sem, t + 1)
                squared.by(act.activation(K.h2[:, t, :], K.res[:, t, :], ACT.Square, accum_out=K.rstd[:, t:t + 1]))
                act.wait_ge(ms.sem, t + 1)
                root.by(act.activation(K.rstd[:, t:t + 1], K.rstd[:, t:t + 1], ACT.Sqrt))
            for k in range(KD):
                act.wait_ge(turned.sem, k + 1)
                moved.by(act.activation(K.h[:, k, :], K.bank[k % 4], ACT.Copy))

        @block.vector
        def _(dve):
            yg = groups(y)
            link(dve, dve.tensor_reduce(mean[:, :], yg, AX.X, ALU.add), K.dve_step)
            link(dve, dve.tensor_scalar(mean[:, :], mean[:, :], 1.0 / 64, None, ALU.mult), K.dve_step)
            link(dve, dve.tensor_tensor(yg, yg, spread_group(mean[:, :]), ALU.subtract), K.dve_step)
            link(dve, dve.tensor_tensor(sq[:, :, :], y, y, ALU.mult), K.dve_step)
            link(dve, dve.tensor_reduce(rstd[:, :], groups(sq[:, :, :]), AX.X, ALU.add), K.dve_step)
            link(dve, dve.tensor_scalar(rstd[:, :], rstd[:, :], 1.0 / 64, GN_EPS, ALU.mult, ALU.add), gvar)
            dve.wait_ge(groot.sem, 1)
            link(dve, dve.reciprocal(rstd[:, :], rstd[:, :]), K.dve_step)
            gnormed.by(dve.tensor_tensor(yg, yg, spread_group(rstd[:, :]), ALU.mult))
            for n, (kind, m) in enumerate(units):
                if kind == "turn":
                    read(dve, n)
                    link(dve, dve.tensor_tensor(rw[:, m, :], rw[:, m, :], bonus[:, m, :], ALU.add), K.dve_step)
                    rw_ready.by(dve.tensor_tensor(rw[:, m, :], rw[:, m, :], gate[:, m, :], ALU.mult))
                if kind == "at":
                    dve.wait_ge(summed.sem, n + 1)
                    dve_out.by(dve.tensor_tensor(sga[:, m, :], sga[:, m, :], K.bank[n % 8], ALU.mult))
                if kind == "rw":
                    dve.wait_ge(summed.sem, n + 1)
                    link(dve, dve.tensor_tensor(sgr[:, m, :], sgr[:, m, :], K.bank[n % 8], ALU.mult), dve_out)
                    mixed.by(dve.tensor_tensor(sga[:, m, :], sga[:, m, :], sgr[:, m, :], ALU.add))
            for t in range(NT):
                x = K.res[:, t, :]
                dve.wait_ge(mm.sem, t + 1)
                link(dve, dve.tensor_tensor(gated[:, :], K.psum[:, D * t:D * t + D], K.arow[:, 0, :], ALU.mult), K.dve_step)
                link(dve, dve.tensor_tensor(x, x, gated[:, :], ALU.add), x2)
                dve.wait_ge(squared.sem, t + 1)
                link(dve, dve.tensor_scalar(K.rstd[:, t:t + 1], K.rstd[:, t:t + 1], 1.0 / D, RMS_EPS, ALU.mult, ALU.add), ms)
                dve.wait_ge(root.sem, t + 1)
                link(dve, dve.reciprocal(K.rstd[:, t:t + 1], K.rstd[:, t:t + 1]), K.dve_step)
                link(dve, dve.scalar_tensor_tensor(out=K.h2[:, t, :], in0=x, scalar=K.rstd[:, t:t + 1], in1=K.arow[:, 2, :], op0=ALU.mult, op1=ALU.mult), K.dve_step)
                scaled.by(dve.tensor_tensor(K.h2[:, t, :], K.h2[:, t, :], K.arow[:, 1, :], ALU.add))
    K.memory.release("sq_gn", "gated3", "h2", "gn_mean", "gn_rstd", "z2", "att2")


EXPERTS, GROUPS, TOP_GROUPS, TOP = 64, 8, 4, 8
E_FF = 256
BLOCK = P
BLOCKS = 96
UNROLL = 3
BIG = 1.0e30
RC_LOWER, RC_TOKEN, RC_BLOCK, RC_STEPS, RC_N = 0, 64, 68, 69, 101


def phase_route(nc, K, ctx):
    d, sb, sig = K.dram, K.buffer, K.flag
    w_r, bias, const, tri = sb("router_w", [P, KD, EXPERTS]), sb("router_bias", [P, EXPERTS]), sb("route_const", [P, RC_N]), sb("tri", [P, P])
    K.shared = sb("shared", [P, NT, D])
    K.weight, slot_f = sb("weight", [P, NT, TOP]), sb("slot_f", [P, NT, TOP])
    K.slot = sb("slot", [P, NT * TOP]).bitcast(U32)
    K.table = sb("block_table", [1, BLOCKS + 8]).bitcast(I32)
    K.tok = sb("block_tokens", [P, BLOCKS + 8]).bitcast(U32)
    sc, ch, tmp, sel = (sb(n, [P, NT, EXPERTS]) for n in ("r_score", "r_choice", "r_tmp", "r_sel"))
    top2, gs, gsel = sb("r_top2", [P, NT * GROUPS, 8]), sb("r_gs", [P, NT, GROUPS]), sb("r_gsel", [P, NT, GROUPS])
    cmp_, cmp2 = sb("r_cmp", [P, NT, GROUPS * GROUPS]), sb("r_cmp2", [P, NT, GROUPS * GROUPS])
    top, tot = sb("r_top", [P, NT, TOP]), sb("r_tot", [P, NT])
    eq = sb("r_eq", [P, TOP, EXPERTS])
    blk, bend = sb("r_blk", [P, EXPERTS]), sb("r_bend", [P, EXPERTS])
    ones = sb("r_ones", [P, EXPERTS])
    eb, trips = sb("r_eb", [P, 8]), sb("r_trips", [P, 32])
    zeros, lists = sb("r_zero", [BLOCKS + 1, P]), sb("r_lists", [BLOCKS + 1, P])
    act_h = sb("shared_h", [P, 2, T])
    hg = sb("shared_g", [P, 2, T])
    small, lg_mm, expo, r_step = sig("router_landed"), sig("logits_summed"), sig("router_exp"), sig("route_step")
    selected, cnt_mm, eb_done, eb_t = (sig(n) for n in ("selected", "counts_summed", "block_experts", "block_experts_turned"))
    slots_done, zeroed, list_t = sig("slots_ready"), sig("zeros_ready"), sig("lists_turned")
    zero_out, scat, list_in = (K.dma_signal(n) for n in ("table_zeroed", "tokens_scattered", "lists_landed"))
    gu_mm, sg_act, sh_mul, dn_mm, sh_out = (sig(n) for n in ("shared_gu", "shared_silu", "shared_product", "shared_down", "shared_out"))
    grp = lambda ap: ap.rearrange("p t (g e) -> p (t g) e", e=EXPERTS // GROUPS)
    steps_at = BLOCKS
    K.steps_at = steps_at

    with nc.Block() as block:
        @block.sync
        def _(sp):
            small.by(sp.dma_start(w_r[:, :, :], d["router_w"].rearrange("p (k e) -> p k e", e=EXPERTS)), 16)
            small.by(sp.dma_start(bias[:, :], d["router_bias"].partition_broadcast(P)), 16)
            small.by(sp.dma_start(const[:, :], d["route_const"]), 16)
            small.by(sp.dma_start(tri[:, :], d["masks"][:, M_S, :]), 16)
            stream(K, sp, d["sh_gu"])
            stream(K, sp, d["sh_down"])

        @block.tensor
        def _(pe):
            pe.wait_ge(small.sem, 64)
            for t in range(NT):
                for k in range(KD):
                    last = pe.matmul(K.bank[0][:, EXPERTS * t:EXPERTS * t + EXPERTS], K.h[:, k, P * t:P * t + P], w_r[:, k, :], start=(k == 0), stop=(k == KD - 1))
            lg_mm.by(last)
            w = take(K, pe).rearrange("p (k m) -> p k m", k=KD)
            for m in range(4):
                for k in range(KD):
                    last = pe.matmul(K.bank[4 + m], w[:, k, P * m:P * m + P], K.h[:, k, :], start=(k == 0), stop=(k == KD - 1))
                gu_mm.by(last)
            free(K, gu_mm)
            pe.wait_ge(selected.sem, 1)
            for t in range(NT):
                out = K.bank[1][:, EXPERTS * t:EXPERTS * t + EXPERTS]
                for b in range(t):
                    pe.matmul(out, K.ones[:, :], sel[:, b, :], start=(b == 0), stop=False)
                pe.matmul(out, tri[:, :], sel[:, t, :], start=(t == 0), stop=True)
            for t in range(NT):
                last = pe.matmul(K.bank[2][:, 0:EXPERTS], K.ones[:, :], sel[:, t, :], start=(t == 0), stop=(t == NT - 1))
            cnt_mm.by(last)
            w = take(K, pe)[:, 0:2 * D].rearrange("p (k n) -> p k n", k=2)
            pe.wait_ge(sh_mul.sem, 2)
            for n in range(2 * NT):
                t, half = divmod(n, 2)
                if n >= 2:
                    pe.wait_ge(sh_out.sem, n - 1)
                for k in range(2):
                    last = pe.matmul(K.bank[6 + n % 2], act_h[:, k, P * t:P * t + P], w[:, k, 512 * half:512 * half + 512], start=(k == 0), stop=(k == 1))
                dn_mm.by(last)
            free(K, dn_mm)
            pe.wait_ge(eb_done.sem, 1)
            eb_t.by(pe.transpose(K.bank[3][0:8, 0:P], eb[:, :], K.ident[:, :]))
            pe.wait_ge(list_in.sem, 16)
            list_t.by(pe.transpose(K.bank[4][:, 0:BLOCKS + 1], lists[:, :], K.ident[0:BLOCKS + 1, 0:BLOCKS + 1]))

        @block.scalar
        def _(act):
            act.wait_ge(lg_mm.sem, 1)
            expo.by(act.activation(sc[:, :, :].rearrange("p t e -> p (t e)"), K.bank[0][:, 0:NT * EXPERTS], ACT.Exp, scale=-1.0))
            for m in range(2):
                act.wait_ge(gu_mm.sem, m + 1)
                sg_act.by(act.activation(hg[:, m, :], K.bank[4 + m], ACT.Silu))
            for n in range(2 * NT):
                t, half = divmod(n, 2)
                act.wait_ge(dn_mm.sem, n + 1)
                sh_out.by(act.activation(K.shared[:, t, 512 * half:512 * half + 512], K.bank[6 + n % 2], ACT.Copy))

        @block.gpsimd
        def _(pool):
            zeroed.by(pool.memset(zeros[:, :], 0.0))
            pool.wait_ge(zeroed.sem, 1)
            zero_out.by(pool.dma_start(d["slot_tokens"].rearrange("(b s) n -> b (s n)", s=BLOCK), zeros[:, :]), 16)
            pool.wait_ge(zero_out.sem, 16)
            pool.wait_ge(small.sem, 64)
            pool.wait_ge(slots_done.sem, 1)
            for t in range(NT):
                for j in range(TOP):
                    n = TOP * t + j
                    scat.by(pool.indirect_dma_start(d["slot_tokens"], bass.IndirectOffsetOnAxis(ap=K.slot[:, n:n + 1], axis=0),
                                                    const[:, RC_TOKEN + t:RC_TOKEN + t + 1], None), 16)
            pool.wait_ge(scat.sem, scat.n)
            list_in.by(pool.dma_start(lists[:, :], d["slot_tokens"].rearrange("(b s) n -> b (s n)", s=BLOCK)), 16)

        @block.vector
        def _(dve):
            step = lambda ins: link(dve, ins, r_step)
            tt, ts = dve.tensor_tensor, dve.tensor_scalar
            link(dve, dve.memset(ones[:, :], 1.0), r_step)
            dve.wait_ge(small.sem, 64)
            dve.wait_ge(expo.sem, 1)
            step(ts(sc[:, :, :], sc[:, :, :], 1.0, None, ALU.add))
            step(dve.reciprocal(sc[:, :, :], sc[:, :, :]))
            step(tt(ch[:, :, :], sc[:, :, :], bias[:, :].unsqueeze(1).to_broadcast([P, NT, EXPERTS]), ALU.add))
            for n in range(NT * GROUPS):
                last = dve.max(top2[:, n, :], grp(ch[:, :, :])[:, n, :])
                r_step.by(last)
            dve.wait_ge(r_step.sem, r_step.n)
            step(tt(gs[:, :, :].rearrange("p t g -> p (t g)"), top2[:, :, 0], top2[:, :, 1], ALU.add))
            for t in range(NT):
                mine = gs[:, t, :].unsqueeze(2).to_broadcast([P, GROUPS, GROUPS])
                other = gs[:, t, :].unsqueeze(1).to_broadcast([P, GROUPS, GROUPS])
                c1, c2 = (x[:, t, :].rearrange("p (g o) -> p g o", o=GROUPS) for x in (cmp_, cmp2))
                step(tt(c1, other, mine, ALU.is_gt))
                step(tt(c2, other, mine, ALU.is_equal))
            lower = const[:, RC_LOWER:RC_LOWER + 64].unsqueeze(1).to_broadcast([P, NT, 64])
            step(tt(cmp2[:, :, :], cmp2[:, :, :], lower, ALU.mult))
            step(tt(cmp_[:, :, :], cmp_[:, :, :], cmp2[:, :, :], ALU.add))
            g1 = gsel[:, :, :].rearrange("p t g -> p (t g)")
            step(dve.tensor_reduce(g1, cmp_[:, :, :].rearrange("p t (g o) -> p (t g) o", o=GROUPS), AX.X, ALU.add))
            step(ts(g1, g1, TOP_GROUPS - 0.5, None, ALU.is_lt))
            spread_g = lambda ap: ap.unsqueeze(2).to_broadcast([P, NT * GROUPS, EXPERTS // GROUPS])
            step(tt(grp(ch[:, :, :]), grp(ch[:, :, :]), spread_g(g1), ALU.mult))
            step(ts(g1, g1, -1.0, BIG, ALU.add, ALU.mult))
            step(tt(grp(ch[:, :, :]), grp(ch[:, :, :]), spread_g(g1), ALU.add))
            for t in range(NT):
                step(dve.max(top[:, t, :], ch[:, t, :]))
                step(dve.match_replace(tmp[:, t, :], top[:, t, :], ch[:, t, :], TAKEN))
            link(dve, tt(sel[:, :, :], tmp[:, :, :], ch[:, :, :], ALU.not_equal), selected)
            step(tt(sc[:, :, :], sc[:, :, :], sel[:, :, :], ALU.mult))
            step(dve.tensor_reduce(tot[:, :], sc[:, :, :], AX.X, ALU.add))
            step(dve.reciprocal(tot[:, :], tot[:, :]))
            step(ts(tot[:, :], tot[:, :], 2.5, None, ALU.mult))
            step(tt(sc[:, :, :], sc[:, :, :], tot[:, :].unsqueeze(2).to_broadcast([P, NT, EXPERTS]), ALU.mult))
            dve.wait_ge(cnt_mm.sem, 1)
            cnt = K.bank[2][:, 0:EXPERTS]
            step(ts(blk[:, :], cnt, 0.5, None, ALU.is_gt))
            for k in range(1, T // BLOCK):
                step(dve.scalar_tensor_tensor(out=blk[:, :], in0=cnt, scalar=BLOCK * k + 0.5, in1=blk[:, :], op0=ALU.is_gt, op1=ALU.add))
            step(dve.tensor_tensor_scan(bend[:, :], ones[:, :], blk[:, :], 0.0, ALU.mult, ALU.add))
            step(ts(eb[:, :], ones[:, 0:8], 0.0, None, ALU.mult))
            step(ts(eq[:, 0, :], bend[:, :], const[:, RC_BLOCK:RC_BLOCK + 1], None, ALU.is_le))
            step(dve.tensor_reduce(eb[:, 0:1], eq[:, 0, :], AX.X, ALU.add))
            link(dve, ts(eb[:, 0:1], eb[:, 0:1], EXPERTS - 1.0, None, ALU.min), eb_done)
            step(ts(trips[:, :], const[:, RC_STEPS:RC_STEPS + 32], bend[:, EXPERTS - 1:EXPERTS], None, ALU.is_lt))
            step(dve.tensor_reduce(tot[:, 0:1], trips[:, :], AX.X, ALU.add))
            step(ts(tot[:, 0:1], tot[:, 0:1], -1.0, None, ALU.add))
            step(tt(blk[:, :], bend[:, :], blk[:, :], ALU.subtract))
            step(ts(blk[:, :], blk[:, :], float(BLOCK), 1.0, ALU.mult, ALU.add))
            step(tt(tmp[:, :, :], K.bank[1][:, 0:NT * EXPERTS].rearrange("p (t e) -> p t e", e=EXPERTS), blk[:, :].unsqueeze(1).to_broadcast([P, NT, EXPERTS]), ALU.add))
            step(tt(tmp[:, :, :], tmp[:, :, :], sel[:, :, :], ALU.mult))
            for t in range(NT):
                step(dve.max(slot_f[:, t, :], tmp[:, t, :]))
            link(dve, ts(K.slot[:, :], slot_f[:, :, :].rearrange("p t j -> p (t j)"), -1.0, None, ALU.add), slots_done)
            for t in range(NT):
                a = tmp[:, t, :].unsqueeze(1).to_broadcast([P, TOP, EXPERTS])
                b = slot_f[:, t, :].unsqueeze(2).to_broadcast([P, TOP, EXPERTS])
                step(tt(eq[:, :, :], a, b, ALU.is_equal))
                step(tt(eq[:, :, :], eq[:, :, :], sc[:, t, :].unsqueeze(1).to_broadcast([P, TOP, EXPERTS]), ALU.mult))
                step(dve.tensor_reduce(K.weight[:, t, :], eq[:, :, :], AX.X, ALU.add))
            for m in range(2):
                dve.wait_ge(sg_act.sem, m + 1)
                dve.wait_ge(gu_mm.sem, m + 3)
                sh_mul.by(tt(act_h[:, m, :], hg[:, m, :], K.bank[6 + m], ALU.mult))
            dve.wait_ge(eb_t.sem, 1)
            step(dve.tensor_copy(K.table[:, 0:BLOCKS], K.bank[3][0:1, 0:BLOCKS]))
            step(dve.tensor_copy(K.table[:, steps_at:steps_at + 1], tot[0:1, 0:1]))
            dve.wait_ge(list_t.sem, 1)
            step(dve.tensor_copy(K.tok[:, 0:BLOCKS + 1], K.bank[4][:, 0:BLOCKS + 1]))
    K.memory.release("router_w", "router_bias", "route_const", "tri", "slot_f", "r_score", "r_choice", "r_tmp", "r_sel", "r_top2", "r_gs", "r_gsel",
                     "r_cmp", "r_cmp2", "r_top", "r_tot", "r_eq", "r_blk", "r_bend", "r_ones", "r_eb", "r_trips", "r_zero", "r_lists", "shared_h",
                     "shared_g", "h", "row", "ws")


def phase_experts(nc, K, ctx):
    d, sb, sig = K.dram, K.buffer, K.flag
    U = UNROLL
    gu, down = sb("e_gu", [P, U, KD * 2 * E_FF]), sb("e_down", [P, U, 2 * D])
    xg, xt = sb("e_x", [P, U, D]), sb("e_xt", [P, U, D])
    g, h, ht, out = sb("e_g", [P, U, E_FF]), sb("e_h", [P, U, E_FF]), sb("e_ht", [P, U, E_FF]), sb("e_out", [P, U, D])
    rows = sb("e_rows", [P, 8]).bitcast(U32)
    wait_for = sb("e_wait_for", [P, 8])
    row_step = sig("e_rows_ready")
    gu_in, down_in, out_dma = ([sig(f"{n}{s}") for s in range(U)] for n in ("e_gu_landed", "e_down_landed", "e_out_stored"))
    x_in = [K.dma_signal(f"e_x_landed{s}") for s in range(U)]
    turned, xt_act, xt_dve = sig("e_x_turned"), sig("e_xt_by_act"), sig("e_xt_by_dve")
    gu_mm, silu, product = sig("e_gu_summed"), sig("e_silu"), sig("e_product")
    h_turned, ht_out = sig("e_h_turned"), sig("e_ht_written")
    down_mm, out_act, out_dve = sig("e_down_summed"), sig("e_out_by_act"), sig("e_out_by_dve")
    table = K.table

    def steps(engine, step, last=None):
        more = engine.value_load(table[0:1, K.steps_at:K.steps_at + 1], min_val=1, max_val=BLOCKS // U - 1)
        for s in range(2 * U):
            step(s // U, s % U)
        with engine.Fori(2, more + 1) as i:
            for s in range(U):
                step(i, s)
        if last:
            last(more)

    def blocks_done(engine, signal, i, s, off):
        first = s + off + 1
        if isinstance(i, int):
            if U * i + first > 0:
                engine.wait_ge(signal.sem, U * i + first)
        else:
            engine.wait_ge(signal.sem, i * U + first)

    def landed(engine, signals, i, s, off):
        at = s + off
        if isinstance(i, int):
            if i + at // U + 1 > 0:
                engine.wait_ge(signals[at % U].sem, 16 * (i + at // U + 1))
        else:
            engine.wait_ge(signals[at % U].sem, i * 16 + 16 * (at // U + 1))

    def at(i, n):
        return bass.ds(i * U + n, 1) if not isinstance(i, int) else slice(U * i + n, U * i + n + 1)

    with nc.Block() as block:
        @block.tensor
        def _(pe):
            def turn_x(i, s, off):
                b = (s + off) % U
                landed(pe, x_in, i, s, off)
                blocks_done(pe, xt_act, i, s, off - 1)
                blocks_done(pe, xt_dve, i, s, off - 1)
                for k in range(KD):
                    last = pe.transpose(K.psum[:, P * k:P * k + P], xg[:, b, P * k:P * k + P], K.ident[:, :])
                last.then_inc(turned.sem, 1)

            def down_products(i, s):
                b = (s - 1) % U
                blocks_done(pe, ht_out, i, s, -1)
                landed(pe, down_in, i, s, -1)
                blocks_done(pe, out_act, i, s, -2)
                blocks_done(pe, out_dve, i, s, -2)
                for half in range(2):
                    for k in range(2):
                        last = pe.matmul(K.bank[5 + half], ht[:, b, P * k:P * k + P], down[:, b, D * k + 512 * half:D * k + 512 * half + 512],
                                         start=(k == 0), stop=(k == 1))
                last.then_inc(down_mm.sem, 1)

            def step(i, s):
                turn_x(i, s, 1)
                landed(pe, gu_in, i, s, 0)
                for k in range(KD):
                    last = pe.matmul(K.bank[2 + s], xt[:, s, P * k:P * k + P], gu[:, s, 2 * E_FF * k:2 * E_FF * (k + 1)], start=(k == 0), stop=(k == KD - 1))
                last.then_inc(gu_mm.sem, 1)
                if not (isinstance(i, int) and i + s == 0):
                    down_products(i, s)
                blocks_done(pe, product, i, s, 0)
                for k in range(2):
                    last = pe.transpose(K.bank[7][:, P * k:P * k + P], h[:, s, P * k:P * k + P], K.ident[:, :])
                last.then_inc(h_turned.sem, 1)

            turn_x(0, 0, 0)
            steps(pe, step, lambda n: down_products(n, U))

        @block.scalar
        def _(act):
            def move_x(i, s, off):
                blocks_done(act, turned, i, s, off)
                blocks_done(act, gu_mm, i, s, off - U)
                act.activation(xt[:, (s + off) % U, 0:512], K.bank[0], ACT.Copy).then_inc(xt_act.sem, 1)

            def move_out(i, s):
                blocks_done(act, down_mm, i, s, -1)
                landed(act, out_dma, i, s, -1 - U)
                act.activation(out[:, (s - 1) % U, 0:512], K.bank[5], ACT.Copy).then_inc(out_act.sem, 1)

            def step(i, s):
                move_x(i, s, 1)
                blocks_done(act, gu_mm, i, s, 0)
                blocks_done(act, product, i, s, -U)
                act.activation(g[:, s, :], K.bank[2 + s][:, 0:E_FF], ACT.Silu).then_inc(silu.sem, 1)
                if not (isinstance(i, int) and i + s == 0):
                    move_out(i, s)
                blocks_done(act, h_turned, i, s, 0)
                act.activation(ht[:, s, :], K.bank[7][:, 0:E_FF], ACT.Copy).then_inc(ht_out.sem, 1)

            def rest(n):
                move_out(n, U)
                for s in range(U):
                    act.wait_ge(out_dma[s].sem, n * 16 + 16)
                    act.activation(g[:, 0, s:s + 1], K.rstd[:, 0:1], ACT.Copy)

            move_x(0, 0, 0)
            steps(act, step, rest)

        @block.vector
        def _(dve):
            def move_x(i, s, off):
                blocks_done(dve, turned, i, s, off)
                blocks_done(dve, gu_mm, i, s, off - U)
                dve.tensor_copy(xt[:, (s + off) % U, 512:D], K.bank[1]).then_inc(xt_dve.sem, 1)

            def move_out(i, s):
                blocks_done(dve, down_mm, i, s, -1)
                landed(dve, out_dma, i, s, -1 - U)
                dve.tensor_copy(out[:, (s - 1) % U, 512:D], K.bank[6]).then_inc(out_dve.sem, 1)

            def step(i, s):
                move_x(i, s, 1)
                blocks_done(dve, silu, i, s, 0)
                blocks_done(dve, h_turned, i, s, -U)
                dve.tensor_tensor(h[:, s, :], g[:, s, :], K.bank[2 + s][:, E_FF:2 * E_FF], ALU.mult).then_inc(product.sem, 1)
                if not (isinstance(i, int) and i + s == 0):
                    move_out(i, s)

            move_x(0, 0, 0)
            steps(dve, step, lambda n: move_out(n, U))

        @block.gpsimd
        def _(pool):
            def gather(i, s, off):
                blocks_done(pool, turned, i, s, off - U)
                b = (s + off) % U
                pool.tensor_copy(rows[:, b:b + 1], K.tok[:, at(i, s + off)]).then_inc(row_step.sem, 1)
                blocks_done(pool, row_step, i, s, off)
                pool.tensor_tensor(wait_for[:, b:b + 1], K.rstd[:, 0:1], K.rstd[:, 0:1], ALU.add)
                pool.indirect_dma_start(xg[:, b, :], None, d["h2"], bass.IndirectOffsetOnAxis(ap=rows[:, b:b + 1], axis=0)).then_inc(x_in[b].sem, 16)

            gather(0, 0, 0)
            steps(pool, lambda i, s: gather(i, s, 1))

        @block.sync
        def _(sp):
            def store(i, s, off):
                blocks_done(sp, out_act, i, s, off)
                blocks_done(sp, out_dve, i, s, off)
                b = (s + off) % U
                dst = d["expert_out"][at(i, s + off)].rearrange("a p n -> (a p) n")
                sp.dma_start(dst, out[:, b, :]).then_inc(out_dma[b].sem, 16)

            def step(i, s):
                e = sp.value_load(table[0:1, at(i, s)], min_val=0, max_val=EXPERTS - 1)
                blocks_done(sp, down_mm, i, s, -U)
                sp.dma_start(gu[:, s, :], d["exp_gu"][bass.ds(e, 1)].rearrange("a p n -> (a p) n")).then_inc(gu_in[s].sem, 16)
                sp.dma_start(down[:, s, :], d["exp_down"][bass.ds(e, 1)].rearrange("a p n -> (a p) n")).then_inc(down_in[s].sem, 16)
                if not isinstance(i, int) or i > 0:
                    store(i, s, -U)

            def rest(n):
                for s in range(U):
                    store(n, s, 0)


            steps(sp, step, rest)
    K.memory.release("e_gu", "e_down", "e_x", "e_xt", "e_g", "e_h", "e_ht", "e_out", "e_rows", "e_wait_for")


def phase_combine(nc, K, ctx):
    d, sb, sig = K.dram, K.buffer, K.flag
    RING = 8
    yg, out, gated = sb("c_rows", [P, RING, D]), sb("c_out", [P, NT, D]), sb("c_gated", [P, D])
    frow = sb("final_row", [P, D])
    sem_in = [K.dma_signal(f"c_landed{n}") for n in range(RING)]
    row_in, used, x3, squared, ms, root, done, stored = (sig(n) for n in ("final_landed", "c_used", "x3", "x3_squared", "x3_ms", "x3_root", "out_ready", "out_stored"))

    with nc.Block() as block:
        @block.gpsimd
        def _(pool):
            for n in range(NT * TOP):
                if n >= RING:
                    pool.wait_ge(used.sem, n - RING + 1)
                sem_in[n % RING].by(pool.indirect_dma_start(yg[:, n % RING, :], None, d["expert_out"].rearrange("b p n -> (b p) n"),
                                                            bass.IndirectOffsetOnAxis(ap=K.slot[:, n:n + 1], axis=0)), 16)

        @block.vector
        def _(dve):
            for t in range(NT):
                x, s = K.res[:, t, :], K.shared[:, t, :]
                for j in range(TOP):
                    n = TOP * t + j
                    dve.wait_ge(sem_in[n % RING].sem, 16 * (n // RING + 1))
                    link(dve, dve.scalar_tensor_tensor(out=s, in0=yg[:, n % RING, :], scalar=K.weight[:, t, j:j + 1], in1=s, op0=ALU.mult, op1=ALU.add), used)
                link(dve, dve.tensor_tensor(gated[:, :], s, K.arow[:, 3, :], ALU.mult), K.dve_step)
                link(dve, dve.tensor_tensor(x, x, gated[:, :], ALU.add), x3)
                dve.wait_ge(squared.sem, t + 1)
                link(dve, dve.tensor_scalar(K.rstd[:, t:t + 1], K.rstd[:, t:t + 1], 1.0 / D, RMS_EPS, ALU.mult, ALU.add), ms)
                dve.wait_ge(root.sem, t + 1)
                link(dve, dve.reciprocal(K.rstd[:, t:t + 1], K.rstd[:, t:t + 1]), K.dve_step)
                dve.wait_ge(row_in.sem, 16)
                done.by(dve.scalar_tensor_tensor(out=out[:, t, :], in0=x, scalar=K.rstd[:, t:t + 1], in1=frow[:, :], op0=ALU.mult, op1=ALU.mult))

        @block.scalar
        def _(act):
            for t in range(NT):
                act.wait_ge(x3.sem, t + 1)
                squared.by(act.activation(out[:, t, :], K.res[:, t, :], ACT.Square, accum_out=K.rstd[:, t:t + 1]))
                act.wait_ge(ms.sem, t + 1)
                root.by(act.activation(K.rstd[:, t:t + 1], K.rstd[:, t:t + 1], ACT.Sqrt))

        @block.sync
        def _(sp):
            row_in.by(sp.dma_start(frow[:, :], d["rows"][ROWS.index("final_g_2")].partition_broadcast(P)), 16)
            for t in range(NT):
                sp.wait_ge(done.sem, t + 1)
                stored.by(sp.dma_start(d["out"][P * t:P * t + P, :], out[:, t, :]), 16)
            sp.wait_ge(stored.sem, stored.n)


PHASES = [phase_modulate, phase_project, phase_mix, phase_output, phase_ffn_up, phase_ffn_down, phase_in2, phase_sparse, phase_recur, phase_branches, phase_route, phase_experts, phase_combine]


def build(nc, d, upto=99):
    d["w_in"] = [d["w_in0"][0], d["w_in0"][1], d["w_in_q"], d["w_in_kv"]]
    with ExitStack() as ctx, ExitStack() as owner:
        K = setup(nc, ctx, d)
        K.own = []
        for n, phase in enumerate(PHASES[:upto]):
            if n in (0, 5, 9):
                new_signals(nc, K, owner, ctx)
            phase(nc, K, ctx)
        if upto < 99:
            with nc.Block() as block:
                @block.sync
                def _(sp):
                    for x in K.ws_landed:
                        sp.wait_ge(x.sem, x.n)
    return K


SCRATCH = {"gate_rows": (2, 2 * KD, P), "toe_line": (HEADS, TOE), "toe_wide": (P * HEADS * TOE + P,), "h2": (T, D), "slot_tokens": ((BLOCKS + 1) * BLOCK, 1), "expert_out": (BLOCKS, BLOCK, D)}


def _columns(v):
    return np.ascontiguousarray(np.reshape(v, (-1, P)).T)


def _tiles(w, size):
    inner, outer = w.shape
    w = w.reshape(inner // P, P, outer // size, size)
    return np.ascontiguousarray(w.transpose(2, 1, 0, 3)).reshape(outer // size, P, -1)


def _rows(w, size):
    inner, outer = w.shape
    w = w.reshape(inner // P // size, size, P, outer)
    return np.ascontiguousarray(w.transpose(0, 2, 1, 3)).reshape(inner // P // size, P, -1)


def _swapped(n):
    return np.concatenate([np.arange(n // 2, n), np.arange(n // 2)])


def _rope_tables():
    rows = np.arange(T) // 64
    cols_ = np.arange(T) % 64
    n_freq = QK_ROPE // 4
    inv = np.float32(10000.0) ** (-np.arange(n_freq, dtype=np.float32) / np.float32(n_freq))
    ang = np.concatenate([rows[:, None].astype(np.float32) * inv, cols_[:, None].astype(np.float32) * inv], axis=-1)
    cos, sin = np.cos(ang).T, np.sin(ang).T
    c, s = np.concatenate([cos, cos]), np.concatenate([-sin, sin])
    return np.ascontiguousarray(np.stack([np.concatenate([c] * 4), np.concatenate([s] * 4)], axis=1)).astype(np.float32)


def _bucket_hot():
    n = np.arange(T)
    large = 16 + (np.log(np.maximum(n, 1).astype(np.float32) / np.float32(16)) / np.float32(np.log(128 / 16)) * np.float32(16)).astype(np.int32)
    bucket = np.where(n < 16, n, np.minimum(large, 31))
    hot = np.zeros((33, TOE), np.float32)
    hot[bucket, T - 1 - n] = 1.0
    hot[32, T:] = 1.0
    return hot


def lay_out(**inputs):
    a = {k: np.asarray(v) for k, v in inputs.items()}
    for k in list(a):
        if k not in ("x", "ctx", "c", "c_2", "c_ctx", "rel_bias_2", "final_g_2"):
            a[k] = a[k][0]
    o = {}
    parts = []
    for name in COLS:
        if name == "conv_dw_w":
            parts.append(a[name].reshape(CONV_K, 4, P).transpose(2, 1, 0).reshape(P, -1))
        else:
            parts.append(_columns(a[name].reshape(-1)))
    o["cols"] = np.ascontiguousarray(np.concatenate(parts, axis=1))
    o["rows"] = np.stack([a[n].reshape(-1) for n in ROWS])
    o["ident"] = np.eye(P, dtype=np.float32)
    o["x"], o["ctx"] = a["x"][0], a["ctx"][0]
    o["w_ada"] = _tiles(a["w_ada"], 512)
    w = a["w_in"]
    u, latent = w[:, :2 * C_CONV], w[:, 2 * C_CONV:]
    kr = latent[:, Q_LORA + KV_LORA:]
    groups = [u[:, C_CONV:], u[:, :C_CONV], latent[:, :Q_LORA],
              np.concatenate([latent[:, Q_LORA:Q_LORA + KV_LORA]] + [kr] * 4 + [kr[:, _swapped(QK_ROPE)]] * 4, axis=1)]
    o["w_in0"] = np.concatenate([_tiles(groups[0], 512), _tiles(groups[1], 512)])
    o["w_in_q"] = _tiles(groups[2], Q_LORA)[0]
    o["w_in_kv"] = _tiles(groups[3], 512)[0]
    q = a["w_uq"].reshape(Q_LORA, HEADS, QK_NOPE + QK_ROPE)
    rot = q[:, :, QK_NOPE:]
    o["w_uq"] = _tiles(np.concatenate([q[:, :, :QK_NOPE].reshape(Q_LORA, -1), rot.reshape(Q_LORA, -1),
                                       rot[:, :, _swapped(QK_ROPE)].reshape(Q_LORA, -1)], axis=1), 1024)[0]
    kv = a["w_ukv"].reshape(KV_LORA, HEADS, QK_NOPE + V_DIM)
    o["w_ukv"] = _tiles(np.concatenate([kv[:, :, :QK_NOPE].reshape(KV_LORA, -1), kv[:, :, QK_NOPE:].reshape(KV_LORA, -1)], axis=1), 1024)[0]
    o["rope"] = _rope_tables()
    o["w_o"] = _rows(a["w_o"], 4)
    o["ada_w_2"], o["ada_b_2"] = _tiles(a["ada_w_2"], 512), a["ada_b_2"].reshape(1, 12, 512)
    o["norm2_g"] = a["norm2_g_2"]
    up = a["w_up"].reshape(D, 2, NF, P).transpose(0, 2, 1, 3).reshape(D, -1)
    o["w_up"] = _tiles(up, 2 * P)
    taps = np.concatenate([a["ffn_dw_w"], a["ffn_dw_b"][None]]).reshape(4, 2, NF, P)
    o["ffn_taps"] = np.ascontiguousarray(taps.transpose(2, 3, 1, 0)).reshape(NF, P, 8)
    down = a["w_down"].reshape(NF, P, D)
    last = NF % 4
    down = np.concatenate([down, down[:(4 - last) % 4]])
    o["w_down"] = np.ascontiguousarray(down.reshape(-1, 4, P, D).transpose(0, 2, 1, 3)).reshape(-1, P, 4 * D)
    w = a["w_in_2"]
    cut = np.cumsum([0, 512, 512, 512, 512, 32, 16, 512, 512, 512, 64, 64, 128, D, D])
    q, k, v, iq, ik, iw, r, kk, vv, wd, ad, gd, ga, gr = (w[:, x:y] for x, y in zip(cut[:-1], cut[1:]))
    o["w_in2"] = _tiles(np.concatenate([q, k, iq] + [ik] * 4 + [r, kk, vv, wd, ad, gd] + [iw] * 8, axis=1), 512)
    o["w_v2"] = _tiles(v, 512)[0]
    o["w_gates"] = _tiles(np.concatenate([ga, gr], axis=1), 512)
    o["w_attn_br"], o["w_rwkv_br"] = _tiles(a["w_attn_br_2"], D)[0], _tiles(a["w_rwkv_br_2"], D)[0]
    o["w_out"] = _rows(a["w_out_2"], 4)
    o["router_w"], o["router_bias"] = _tiles(a["router_w_2"], EXPERTS)[0], a["router_bias_2"]
    o["sh_gu"], o["sh_down"] = _tiles(np.concatenate([a["sh_gate_2"], a["sh_up_2"]], axis=1), 2 * E_FF)[0], _tiles(a["sh_down_2"], D)[0]
    const = np.zeros((P, RC_N), np.float32)
    g = np.arange(GROUPS)
    const[:, RC_LOWER:RC_LOWER + 64] = (g[None] < g[:, None]).reshape(-1)
    const[:, RC_TOKEN:RC_TOKEN + NT] = np.arange(T).reshape(NT, P).T
    const[:, RC_BLOCK] = np.arange(P)
    const[:, RC_STEPS:RC_STEPS + BLOCKS // UNROLL] = np.arange(0, BLOCKS, UNROLL)
    o["route_const"] = const
    ff = np.concatenate([a["exp_gate_2"], a["exp_up_2"]], axis=2).reshape(EXPERTS, KD, P, 2 * E_FF)
    o["exp_gu"] = np.ascontiguousarray(ff.transpose(0, 2, 1, 3)).reshape(EXPERTS, P, -1)
    o["exp_down"] = np.ascontiguousarray(a["exp_down_2"].reshape(EXPERTS, 2, P, D).transpose(0, 2, 1, 3)).reshape(EXPERTS, P, -1)
    z64 = np.zeros((64, 512), np.float32)
    o["ups"] = np.stack([np.concatenate([a["decay_up_2"], z64]), np.concatenate([z64, a["iclr_up_2"]]), a["gate_up_2"]], axis=1)
    i, j = np.arange(P)[:, None], np.arange(P)[None]
    same = i // SUB == j // SUB
    o["masks"] = np.stack([same & (i < j), ~same & (i < j), same & (i > j), i < j, i <= j, i // 64 == j // 64], axis=1).astype(np.float32)
    o["rel_bias"], o["bucket_hot"] = a["rel_bias_2"], _bucket_hot()
    return o


def kernel(**inputs):
    import concourse.bacc as bacc
    from concourse.bass_utils import run_bass_kernel_spmd

    nc = bacc.Bacc("TRN2", target_bir_lowering=False, num_devices=1)
    dram, arrays = {}, {}
    for name, a in lay_out(**inputs).items():
        arrays[f"in_{name}"] = a = np.ascontiguousarray(a)
        dram[name] = nc.dram_tensor(f"in_{name}", a.shape, mybir.dt.from_np(a.dtype), kind="ExternalInput").ap()
    for name, shape in SCRATCH.items():
        dram[name] = nc.dram_tensor(f"scratch_{name}", shape, F32).ap()
    dram["out"] = nc.dram_tensor("out", (T, D), F32, kind="ExternalOutput").ap()
    build(nc, dram)
    result = run_bass_kernel_spmd(nc, [arrays], core_ids=[0])
    return result.results[0]["out"].reshape(1, T, D)
```
